# Optimizing a Trainium2 kernel written in Bass

```python
import jax
import jax.numpy as jnp
from jax import lax
import numpy as np

D_MODEL = 2048
BATCH = 1
SEQ = 256
DEPTH = 1

HEAD_DIM = 64
MIX_WIDTH = D_MODEL
A_WIDTH = MIX_WIDTH // 2
B_WIDTH = MIX_WIDTH - A_WIDTH
A_HEADS = A_WIDTH // HEAD_DIM
B_Q_HEADS = B_WIDTH // HEAD_DIM
B_KV_HEADS = max(1, B_Q_HEADS // 8)
B_GROUP = B_Q_HEADS // B_KV_HEADS
KV_B_WIDTH = B_KV_HEADS * HEAD_DIM
QKV_WIDTH = 3 * A_WIDTH + B_WIDTH + 2 * KV_B_WIDTH
DILATED_PATTERNS = ((128, 1), (512, 4), (2048, 16))
SWA_WINDOW = 128
BLOCK = 128
D_FF = ((8 * D_MODEL // 3 + 255) // 256) * 256
PLE_DIM = 256
ALIBI_MAX_BIAS = 8.0
EPS = 1e-6

kernel_name = 'hybrid_dilated_swa_macaron_layer'

def rmsnorm(x, g):
    xf = x.astype(jnp.float32)
    y = xf * lax.rsqrt(jnp.mean(xf * xf, axis=-1, keepdims=True) + EPS)
    return (y * g.astype(jnp.float32)).astype(x.dtype)

def swiglu(x, w_gate, w_up, w_down):
    return (jax.nn.silu(x @ w_gate) * (x @ w_up)) @ w_down

def alibi_slopes(n):
    return jnp.exp2(-ALIBI_MAX_BIAS * (jnp.arange(n, dtype=jnp.float32) + 1.0) / n)

def banded_attention(q, k, v, slopes, dist_scale, window, sinks=None):
    n, hk, g, length, dh = q.shape
    nb = -(-length // BLOCK)
    pad = nb * BLOCK - length
    qb = jnp.pad(q, ((0, 0), (0, 0), (0, 0), (0, pad), (0, 0))).reshape(n, hk, g, nb, BLOCK, dh)

    def band(t):
        t = jnp.pad(t, ((0, 0), (0, 0), (BLOCK, pad), (0, 0))).reshape(n, hk, nb + 1, BLOCK, dh)
        return jnp.concatenate([t[:, :, :-1], t[:, :, 1:]], axis=3)

    kb, vb = band(k), band(v)
    s = jnp.einsum('nhgbqd,nhbkd->nhgbqk', qb, kb).astype(jnp.float32) * (dh ** -0.5)
    qi = jnp.arange(BLOCK)[:, None]
    kj = jnp.arange(2 * BLOCK)[None, :]
    rel = qi + BLOCK - kj
    blk = jnp.arange(nb)[:, None, None]
    valid = (rel >= 0) & (rel <= window) & ((blk > 0) | (kj >= BLOCK))
    bias = -slopes.astype(jnp.float32)[:, :, None, None, None] * (dist_scale * rel).astype(jnp.float32)
    s = jnp.where(valid, s + bias, -jnp.inf)
    m = jnp.max(s, axis=-1, keepdims=True)
    if sinks is not None:
        sk = sinks.astype(jnp.float32)[:, :, None, None, None]
        m = jnp.maximum(m, sk)
    e = jnp.exp(s - m)
    denom = jnp.sum(e, axis=-1, keepdims=True)
    if sinks is not None:
        denom = denom + jnp.exp(sk - m)
    o = jnp.einsum('nhgbqk,nhbkd->nhgbqd', e, vb.astype(jnp.float32)) / denom
    lse = (m + jnp.log(denom))[..., 0]
    o = o.reshape(n, hk, g, nb * BLOCK, dh)[:, :, :, :length]
    lse = lse.reshape(n, hk, g, nb * BLOCK)[:, :, :, :length]
    return o, lse

def dilated_attention(q, k, v, slopes):
    bsz, seq, nh, dh = q.shape
    outs, lses = [], []
    for window, dil in DILATED_PATTERNS:
        sub = seq // dil

        def fold(t):
            return t.reshape(bsz, sub, dil, nh, dh).transpose(0, 2, 3, 1, 4).reshape(bsz * dil, nh, sub, dh)

        o, lse = banded_attention(fold(q)[:, :, None], fold(k), fold(v), slopes[:, None], dil, window // dil)
        outs.append(o[:, :, 0].reshape(bsz, dil, nh, sub, dh).transpose(0, 3, 1, 2, 4).reshape(bsz, seq, nh, dh))
        lses.append(lse[:, :, 0].reshape(bsz, dil, nh, sub).transpose(0, 3, 1, 2).reshape(bsz, seq, nh))
    w = jax.nn.softmax(jnp.stack(lses, axis=0), axis=0)
    out = jnp.sum(w[..., None] * jnp.stack(outs, axis=0), axis=0)
    return out.astype(q.dtype)

def sink_swa_gqa(q, k, v, slopes, sinks):
    bsz, seq, _ = q.shape
    qh = q.reshape(bsz, seq, B_KV_HEADS, B_GROUP, HEAD_DIM).transpose(0, 2, 3, 1, 4)
    kh = k.reshape(bsz, seq, B_KV_HEADS, HEAD_DIM).transpose(0, 2, 1, 3)
    vh = v.reshape(bsz, seq, B_KV_HEADS, HEAD_DIM).transpose(0, 2, 1, 3)
    o, _ = banded_attention(qh, kh, vh, slopes, 1, SWA_WINDOW - 1, sinks)
    return o.transpose(0, 3, 1, 2, 4).reshape(bsz, seq, B_WIDTH).astype(q.dtype)

def setup_inputs(seed: int = 0) -> dict:
    key = jax.random.key(seed)
    keys = jax.random.split(key, 32)
    ctr = [0]

    def nk():
        ctr[0] += 1
        return keys[ctr[0] - 1]

    def w(shape, fan_in):
        return jax.random.normal(nk(), (DEPTH,) + shape, jnp.float32) * (fan_in ** -0.5)

    def gain(n):
        return 1.0 + 0.05 * jax.random.normal(nk(), (DEPTH, n), jnp.float32)

    def small(shape, scale):
        return scale * jax.random.normal(nk(), (DEPTH,) + shape, jnp.float32)

    return {
        'x': jax.random.normal(nk(), (BATCH, SEQ, D_MODEL), jnp.float32),
        'p': jax.random.normal(nk(), (DEPTH, BATCH, SEQ, PLE_DIM), jnp.float32),
        'g_ffn1_pre': gain(D_MODEL),
        'w_ffn1_gate': w((D_MODEL, D_FF), D_MODEL),
        'w_ffn1_up': w((D_MODEL, D_FF), D_MODEL),
        'w_ffn1_down': w((D_FF, D_MODEL), D_FF),
        'g_ffn1_post': gain(D_MODEL),
        'g_mix_pre': gain(D_MODEL),
        'w_qkv': w((D_MODEL, QKV_WIDTH), D_MODEL),
        'b_qkv': small((QKV_WIDTH,), 0.02),
        'attn_sinks': small((B_KV_HEADS, B_GROUP), 1.0),
        'g_out_a': gain(A_WIDTH),
        'g_out_b': gain(B_WIDTH),
        'w_o': w((MIX_WIDTH, D_MODEL), MIX_WIDTH),
        'b_o': small((D_MODEL,), 0.02),
        'g_mix_post': gain(D_MODEL),
        'g_ffn2_pre': gain(D_MODEL),
        'w_ffn2_gate': w((D_MODEL, D_FF), D_MODEL),
        'w_ffn2_up': w((D_MODEL, D_FF), D_MODEL),
        'w_ffn2_down': w((D_FF, D_MODEL), D_FF),
        'g_ffn2_post': gain(D_MODEL),
        'g_ple_pre': gain(D_MODEL),
        'w_ple_gate': w((D_MODEL, D_MODEL), D_MODEL),
        'w_ple_proj': w((PLE_DIM, D_MODEL), PLE_DIM),
        'g_ple_post': gain(D_MODEL),
    }

def reference(x, p, g_ffn1_pre, w_ffn1_gate, w_ffn1_up, w_ffn1_down, g_ffn1_post,
              g_mix_pre, w_qkv, b_qkv, attn_sinks, g_out_a, g_out_b, w_o, b_o, g_mix_post,
              g_ffn2_pre, w_ffn2_gate, w_ffn2_up, w_ffn2_down, g_ffn2_post,
              g_ple_pre, w_ple_gate, w_ple_proj, g_ple_post):
    bsz, seq, _ = x.shape
    slopes = alibi_slopes(A_HEADS + B_Q_HEADS)
    slopes_a = slopes[0::2]
    slopes_b = slopes[1::2].reshape(B_KV_HEADS, B_GROUP)
    splits = [A_WIDTH, 2 * A_WIDTH, 3 * A_WIDTH, 3 * A_WIDTH + B_WIDTH, 3 * A_WIDTH + B_WIDTH + KV_B_WIDTH]
    h = x
    for i in range(DEPTH):
        f = swiglu(rmsnorm(h, g_ffn1_pre[i]), w_ffn1_gate[i], w_ffn1_up[i], w_ffn1_down[i])
        h = h + 0.5 * rmsnorm(f, g_ffn1_post[i])
        u = rmsnorm(h, g_mix_pre[i])
        z = u @ w_qkv[i] + b_qkv[i]
        qa, ka, va, qb, kb, vb = jnp.split(z, splits, axis=-1)
        qa = qa.reshape(bsz, seq, A_HEADS, HEAD_DIM)
        ka = ka.reshape(bsz, seq, A_HEADS, HEAD_DIM)
        va = va.reshape(bsz, seq, A_HEADS, HEAD_DIM)
        oa = dilated_attention(qa, ka, va, slopes_a).reshape(bsz, seq, A_WIDTH)
        ob = sink_swa_gqa(qb, kb, vb, slopes_b, attn_sinks[i])
        o = jnp.concatenate([rmsnorm(oa, g_out_a[i]), rmsnorm(ob, g_out_b[i])], axis=-1)
        o = o @ w_o[i] + b_o[i]
        h = h + rmsnorm(o, g_mix_post[i])
        f = swiglu(rmsnorm(h, g_ffn2_pre[i]), w_ffn2_gate[i], w_ffn2_up[i], w_ffn2_down[i])
        h = h + 0.5 * rmsnorm(f, g_ffn2_post[i])
        gate = jax.nn.sigmoid(rmsnorm(h, g_ple_pre[i]) @ w_ple_gate[i])
        e = p[i] @ w_ple_proj[i]
        h = h + rmsnorm(gate * e, g_ple_post[i])
    return h


_drawn_inputs = setup_inputs


def setup_inputs(seed=0):
    import zlib

    import numpy as np

    out = dict(_drawn_inputs(seed))
    spreads = {}
    factors = {'g_out_b': 2.67,
     'b_o': 4.583,
     'g_ffn2_pre': 2.939,
     'g_ffn2_post': 4.181,
     'g_ple_pre': 17.917,
     'g_out_a': 3.781,
     'g_ple_post': 3.139}
    for name, (base, spread) in spreads.items():
        noise = np.random.default_rng([zlib.crc32(name.encode()), seed]).standard_normal(out[name].shape)
        drawn = base * np.exp(spread * noise) if base else spread * noise
        out[name] = jnp.asarray(drawn.astype(out[name].dtype))
    for name, factor in factors.items():
        out[name] = (out[name] * factor).astype(out[name].dtype)
    return out
```

```python
from contextlib import ExitStack

import concourse.bass as bass
from concourse import mybir

F32 = mybir.dt.float32
F32R = mybir.dt.float32r
BF16 = mybir.dt.bfloat16
I32 = mybir.dt.int32
ALU = mybir.AluOpType
ACT = mybir.ActivationFunctionType
AX = mybir.AxisListType

P = 128
NB = 512
RING = 4
CPS = 2
EPS = 1e-6
HD = 64
BIG = 1e30
VW = HD + 2


def layer_program(nc, x, p, g_ffn1_pre, w_ffn1_gate, w_ffn1_up, w_ffn1_down, g_ffn1_post,
                  g_mix_pre, w_qkv, b_qkv, attn_sinks, g_out_a, g_out_b, w_o, b_o, g_mix_post,
                  g_ffn2_pre, w_ffn2_gate, w_ffn2_up, w_ffn2_down, g_ffn2_post,
                  g_ple_pre, w_ple_gate, w_ple_proj, g_ple_post, out):
    _, S, D = x.shape
    F = w_ffn1_gate.shape[2]
    QKV = w_qkv.shape[2]
    PLE = p.shape[3]
    AW = g_out_a.shape[1]
    AH = AW // HD
    BH = attn_sinks.shape[1] * attn_sinks.shape[2]
    KVH = attn_sinks.shape[1]
    H = AH + BH
    T = S // P
    KC = D // P
    FC = F // P
    NBD = D // NB
    FB = F // NB
    CB = NB // P
    KS, FS = KC // CPS, FC // CPS
    QB, TAIL = QKV // NB, QKV % NB
    PC = PLE // P
    assert T == 2 and PC == CPS and KVH == 2 and CB == 4 and KS % RING == 0 and 2 * FS % RING == 0
    slope = [2.0 ** (-8.0 * (n + 1) / H) for n in range(H)]
    head_slope = slope[0::2] + slope[1::2]

    S_FFN1 = 0
    S_DOWN1 = S_FFN1 + 2 * KS * FB
    S_QKV = S_DOWN1 + NBD * FS
    S_TAIL = S_QKV + QB * KS
    S_WO = S_TAIL + KS
    S_FFN2 = S_WO + NBD * KS
    S_DOWN2 = S_FFN2 + 2 * KS * FB
    S_PROJ = S_DOWN2 + NBD * FS
    S_GATE = S_PROJ + NBD
    S_END = S_GATE + NBD * KS
    B_QKV = 2 * FB + NBD
    B_TAIL = B_QKV + QB
    B_WO = B_TAIL + 1
    B_FFN2 = B_WO + NBD
    B_PROJ = B_FFN2 + 2 * FB + NBD
    B_GATE = B_PROJ + NBD
    BPB = CB // CPS
    U_X1 = 0
    U_H1 = U_X1 + BPB * NBD
    U_MIX = U_H1 + BPB * FB
    U_O = U_MIX + BPB * NBD
    U_X2 = U_O + BPB * NBD
    U_H2 = U_X2 + BPB * NBD
    U_P = U_H2 + BPB * FB
    U_PLE = U_P + 1
    J_IN1, J_POST1, J_MIX, J_OA, J_OB, J_POSTM, J_IN2, J_POST2, J_PLE, J_POSTP = range(10)
    NJOB = 10
    OBLK = AW // NB
    squares = [T * (OBLK if j in (J_OA, J_OB) else NBD) for j in range(NJOB)]
    Q = [sum(squares[:j]) for j in range(NJOB + 1)]
    R_MIX, R_O, R_X2, R_PLE, R_OUT = (NBD * k for k in range(5))
    CREDIT = 2
    KB = 3 * AW + BH * HD
    QH = 3 * AW
    PAIRS_A, PAIRS = AH // 2, H // 2
    GROUP = 4

    def rows(w):
        return w[0].rearrange("(c p) n -> p c n", p=P)

    with ExitStack() as ctx:
        where = [(nc.sbuf_base + 127) // 128 * 128]

        def sb(name, shape, dt=F32):
            size = 4 if dt != BF16 else 2
            for d in shape[1:]:
                size *= d
            t = nc.alloc_sbuf_tensor_at(name, shape, dt, offset=where[0])
            where[0] += (size + 31) // 32 * 32
            return t

        def sem(name):
            return ctx.enter_context(nc.semaphore(name))

        raw = sb("raw", [P, RING, CPS, NB])
        w_high = sb("w_high", [P, RING, CPS, NB], F32R)
        w_rest = sb("w_rest", [P, RING, CPS, NB], F32R)
        x_high = sb("x_high", [P, KC, S], F32R)
        x_rest = sb("x_rest", [P, KC, S], F32R)
        resid = sb("resid", [P, T, D])
        branch = sb("branch", [P, T, D])
        silu_g = branch[:, 0, 0:T * NB].rearrange("p (t n) -> p t n", t=T)
        hidden = branch[:, 1, 0:T * NB].rearrange("p (t n) -> p t n", t=T)
        gain_row = sb("gain_row", [P, 2, NB])
        ident = sb("ident", [P, P])
        NG = 5
        G_FFN1, G_MIX, G_O, G_FFN2, G_PLE = (KC * k for k in range(NG))
        gain_T = sb("gain_T", [P, NG * KC])
        junk = sb("junk", [P, 2, NB], BF16)
        stat = sb("stat", [P, NJOB, T, NBD])
        ssum = sb("ssum", [P, NJOB, T])
        msq = sb("msq", [P, NJOB, T])
        rstd = sb("rstd", [P, NJOB, T])
        minus_half = sb("minus_half", [P, T])
        sinks = sb("sinks", [P, BH])
        spare = sb("spare", [P, 4])
        turns_from = where[0]
        h_high = sb("h_high", [P, FC, S], F32R)
        h_rest = sb("h_rest", [P, FC, S], F32R)
        turns_to = where[0]
        assert turns_to <= nc.sbuf_usable_end
        where[0] = turns_from
        z = sb("z", [P, T, QKV])
        bias_row = sb("bias_row", [P, QKV])
        vals = sb("vals", [P, T, AH + KVH, VW])
        k_swap = sb("k_swap", [P, T, KVH * HD])
        kb_T = sb("kb_T", [P, 2, S])
        qk_T = sb("qk_T", [P, 2, 2, S])
        dist_i = sb("dist_i", [P, 3 * P], I32)
        bits = sb("bits", [P, 3 * P], I32)
        count = sb("count", [P, 3 * P])
        dist_a = sb("dist_a", [P, 3 * P])
        dist_b = sb("dist_b", [P, 3 * P])
        count_T = sb("count_T", [P, 3 * P])
        tmp = sb("tmp", [P, 3 * P])
        score = sb("score", [P, 2, 3 * P])
        prob = sb("prob", [P, 2, 3 * P])
        prob_T = sb("prob_T", [P, 2, 3 * P])
        peak = sb("peak", [P, 2, T])
        neg_peak = sb("neg_peak", [P, 2, T])
        sink_e = sb("sink_e", [P, BH, T])
        denom = sb("denom", [P, T, GROUP])
        assert where[0] <= turns_to
        where[0] = turns_from
        p_sb = sb("p_sb", [P, T, PLE])
        assert where[0] <= turns_from + CPS * S * 4
        p_high = sb("p_high", [P, PC, S], F32R)
        p_rest = sb("p_rest", [P, PC, S], F32R)
        emb = sb("emb", [P, T, D])
        ple_row = sb("ple_row", [P, D])
        sig = sb("sig", [P, T, NB])
        gated = sb("gated", [P, T, NB])
        assert where[0] <= turns_to
        where[0] = turns_from
        gain_in = sb("gain_in", [P, P])

        bank = [ctx.enter_context(nc.psum_tensor(f"bank{i}", [P, NB], F32)) for i in range(8)]
        acc = [bank[0:2], bank[2:4]]
        turn = bank[4:8]

        w_landed = [sem(f"w_landed{k}") for k in range(RING)]
        w_high_done, w_rest_done, w_used = sem("w_high_done"), sem("w_rest_done"), sem("w_used")
        x_landed = [sem(f"x_landed{k}") for k in range(NBD)]
        gains_landed, sinks_landed, p_landed = sem("gains_landed"), sem("sinks_landed"), sem("p_landed")
        row_landed = [sem("row_landed0"), sem("row_landed1")]
        bias_landed, mix_rows_landed = sem("bias_landed"), sem("mix_rows_landed")
        ple_row_landed, out_landed = sem("ple_row_landed"), sem("out_landed")
        pool_step, dve_step = sem("pool_step"), sem("dve_step")
        ident_ready, dist_ready = sem("ident_ready"), sem("dist_ready")
        gain_turned, gain_T_ready = sem("gain_turned"), sem("gain_T_ready")
        resid_ready = sem("resid_ready")
        turned = sem("turned")
        turn_high = sem("turn_high")
        turn_rest = sem("turn_rest")
        silu_ready, hidden_ready = sem("silu_ready"), sem("hidden_ready")
        squared, summed, rstd_ready = sem("squared"), sem("summed"), sem("rstd_ready")
        biased, branch_ready = sem("biased"), sem("branch_ready")
        z_ready, vals_ready = sem("z_ready"), sem("vals_ready")
        count_ready, count_turned, count_T_ready = sem("count_ready"), sem("count_turned"), sem("count_T_ready")
        pair_turned, q_T_ready, k_T_ready = sem("pair_turned"), sem("q_T_ready"), sem("k_T_ready")
        scored, scores_read, peak_found = sem("scored"), sem("scores_read"), sem("peak_found")
        peak_ready, prob_ready, prob_turned = sem("peak_ready"), sem("prob_ready"), sem("prob_turned")
        prob_T_a, prob_T_b = sem("prob_T_a"), sem("prob_T_b")
        weighed, o_ready = sem("weighed"), sem("o_ready")
        emb_ready, sig_ready, gated_ready = sem("emb_ready"), sem("sig_ready"), sem("gated_ready")

        def wait_prob_T(eng, h):
            if h < AH:
                eng.wait_ge(prob_T_a, h + 1)
            else:
                eng.wait_ge(prob_T_b, h - AH + 1)

        def tail_or_block(slot):
            return TAIL if S_TAIL <= slot < S_WO else NB

        block = ctx.enter_context(nc.Block())

        @block.sync
        def _(sp):
            def load(n, k, src):
                if not (isinstance(n, int) and n < RING):
                    sp.wait_ge(w_rest_done, n - (RING - 1))
                sp.dma_start(raw[:, k, :, 0:src.shape[2]], src).then_inc(w_landed[k], 16)

            def load_block(n, w, slots, col, k0=0, s0=0, width=NB):
                v = rows(w)
                for s in range(s0, slots):
                    load(n + s, (k0 + s) % RING, v[:, CPS * s:CPS * s + CPS, bass.ds(col, width)])

            def load_blocks(n0, w, blocks, start):
                with sp.Fori(start, blocks // 2) as j:
                    for h in range(2):
                        load_block(n0 + KS * h + 2 * KS * j, w, KS, 2 * NB * j + NB * h)

            def ffn(n0, wg, wu, s0=0):
                load_block(n0, wg, KS, 0, s0=s0)
                load_block(n0 + KS, wu, KS, 0)
                with sp.Fori(1, FB) as i:
                    load_block(n0 + 2 * KS * i, wg, KS, NB * i)
                    load_block(n0 + KS + 2 * KS * i, wu, KS, NB * i)

            def down(n0, w, gain, blocks):
                with sp.Fori(0, NBD // 2) as j:
                    for h in range(2):
                        sp.wait_ge(branch_ready, CREDIT - 1 + blocks + 2 * j + h)
                        sp.dma_start(gain_row[:, h, :], gain[:, bass.ds(2 * NB * j + NB * h, NB)].to_broadcast([P, NB])
                                     ).then_inc(row_landed[h], 16)
                        load_block(n0 + FS * h + 2 * FS * j, w, FS, 2 * NB * j + NB * h, k0=FS * h)

            xv = x[0].rearrange("(t p) d -> p t d", p=P)
            for nb in range(NBD):
                sp.dma_start(resid[:, :, nb * NB:(nb + 1) * NB],
                             xv[:, :, nb * NB:(nb + 1) * NB]).then_inc(x_landed[nb], 16)
                load(nb, nb, rows(w_ffn1_gate)[:, CPS * nb:CPS * nb + CPS, 0:NB])
            ffn(S_FFN1, w_ffn1_gate, w_ffn1_up, NBD)
            down(S_DOWN1, w_ffn1_down, g_ffn1_post, 0)
            for s in range(RING):
                load(S_QKV + s, s, rows(w_qkv)[:, CPS * s:CPS * s + CPS, 0:NB])
            sp.wait_ge(w_used, S_QKV)
            sp.dma_start(bias_row[:], b_qkv[:, :].to_broadcast([P, QKV])).then_inc(bias_landed, 16)
            load_block(S_QKV, w_qkv, KS, 0, s0=RING)
            load_block(S_QKV + KS, w_qkv, KS, NB)
            load_blocks(S_QKV, w_qkv, QB, 1)
            load_block(S_TAIL, w_qkv, KS, QB * NB, width=TAIL)
            for s in range(RING):
                load(S_WO + s, s, rows(w_o)[:, CPS * s:CPS * s + CPS, 0:NB])
            sp.wait_ge(z_ready, CREDIT + QB + 1)
            sp.dma_start(bias_row[:, 0:D], b_o[:, :].to_broadcast([P, D])).then_inc(mix_rows_landed, 16)
            sp.dma_start(bias_row[:, D:2 * D], g_mix_post[:, :].to_broadcast([P, D])).then_inc(mix_rows_landed, 16)
            load_block(S_WO, w_o, KS, 0, s0=RING)
            load_block(S_WO + KS, w_o, KS, NB)
            load_blocks(S_WO, w_o, NBD, 1)
            ffn(S_FFN2, w_ffn2_gate, w_ffn2_up)
            down(S_DOWN2, w_ffn2_down, g_ffn2_post, 2 * NBD)
            sp.wait_ge(w_used, S_PROJ - FS + 1)
            sp.dma_start(p_sb[:], p[0, 0].rearrange("(t p) e -> p t e", p=P)).then_inc(p_landed, 16)
            for nb in range(NBD):
                load(S_PROJ + nb, nb, rows(w_ple_proj)[:, :, nb * NB:(nb + 1) * NB])
            load_blocks(S_GATE, w_ple_gate, NBD, 0)
            ov = out[0].rearrange("(t p) d -> p t d", p=P)
            for nb in range(NBD):
                sp.wait_ge(resid_ready, R_OUT + nb + 1)
                sp.dma_start(ov[:, :, nb * NB:(nb + 1) * NB],
                             resid[:, :, nb * NB:(nb + 1) * NB]).then_inc(out_landed, 16)
            sp.wait_ge(out_landed, 16 * NBD)

        @block.gpsimd
        def _(pool):
            steps = [0]

            def step(ins):
                steps[0] += 1
                ins.then_inc(pool_step, 1)
                pool.wait_ge(pool_step, steps[0])

            step(nc.gpsimd.memset(ident[:], 0.0))
            nc.gpsimd.affine_select(out=ident[:], in_=ident[:], compare_op=ALU.not_equal, fill=1.0,
                                    base=0, pattern=[[-1, P]], channel_multiplier=1).then_inc(ident_ready, 1)
            step(nc.gpsimd.memset(minus_half[:], -0.5))

            def factor(job):
                by = 4.0 if job in (J_POST1, J_POST2) else 1.0
                width = AW if job in (J_OA, J_OB) else D
                pool.wait_ge(summed, job + 1)
                step(nc.gpsimd.tensor_scalar(msq[:, job, :], ssum[:, job, :], by / width, by * EPS,
                                             ALU.mult, ALU.add))
                nc.gpsimd.tensor_tensor(rstd[:, job, :], msq[:, job, :], minus_half[:], ALU.pow
                                        ).then_inc(rstd_ready, 1)

            factor(J_IN1)
            factor(J_POST1)
            factor(J_MIX)
            pool.wait_ge(w_used, S_QKV)
            nc.gpsimd.iota(dist_i[:, 0:2 * P], [[-1, 2 * P]], base=P, channel_multiplier=1).then_inc(dist_ready, 1)
            nc.gpsimd.iota(dist_i[:, 2 * P:3 * P], [[-1, P]], base=0, channel_multiplier=1).then_inc(dist_ready, 1)
            step(nc.gpsimd.memset(vals[:, :, :, HD:VW], 1.0))
            pool.wait_ge(z_ready, CREDIT + QH // NB)
            for t in range(T):
                nc.gpsimd.tensor_copy(vals[:, t, 0:AH, 0:HD],
                                      z[:, t, 2 * AW:3 * AW].rearrange("p (h d) -> p h d", d=HD)
                                      ).then_inc(vals_ready, 1)
            pool.wait_ge(z_ready, CREDIT + QB + 1)
            for t in range(T):
                nc.gpsimd.tensor_copy(k_swap[:, t, 0:HD], z[:, t, KB + HD:KB + 2 * HD]).then_inc(vals_ready, 1)
                nc.gpsimd.tensor_copy(k_swap[:, t, HD:2 * HD], z[:, t, KB:KB + HD]).then_inc(vals_ready, 1)
                nc.gpsimd.tensor_copy(vals[:, t, AH:AH + KVH, 0:HD],
                                      z[:, t, KB + KVH * HD:KB + 2 * KVH * HD].rearrange("p (h d) -> p h d", d=HD)
                                      ).then_inc(vals_ready, 1)
            for job in (J_OA, J_OB, J_POSTM, J_IN2, J_POST2, J_PLE, J_POSTP):
                factor(job)

        @block.tensor
        def _(pe):
            def use_slot(n, k, high, rest, chunk, pair, first, last, width=NB):
                pe.wait_ge(w_rest_done, n + 1)
                for c in range(CPS):
                    for t in range(T):
                        o = pair[t][:, 0:width]
                        xh = high[:, chunk + c, t * P:(t + 1) * P]
                        xr = rest[:, chunk + c, t * P:(t + 1) * P]
                        nc.tensor.matmul(o, xh, w_high[:, k, c, 0:width], start=first and c == 0, stop=False)
                        nc.tensor.matmul(o, xh, w_rest[:, k, c, 0:width], start=False, stop=False)
                        ins = nc.tensor.matmul(o, xr, w_high[:, k, c, 0:width], start=False,
                                               stop=last and c == CPS - 1)
                ins.then_inc(w_used, 1)

            def turn_chunks(src, banks):
                for j in range(BPB):
                    for c in range(CPS):
                        for t in range(T):
                            ins = nc.tensor.transpose(banks[j][:, (c * T + t) * P:(c * T + t + 1) * P],
                                                      src(t, CPS * j + c), ident[:])
                    ins.then_inc(turned, 1)

            def turn_block(src, u0, nb, sem_, need):
                pe.wait_ge(sem_, need)
                free = u0 + max(0, BPB * (nb - 1))
                if free:
                    pe.wait_ge(turn_rest, free)
                turn_chunks(lambda t, c: src(t, nb * CB + c), turn[BPB * (nb % 2):BPB * (nb % 2) + BPB])

            def resid_chunk(t, c):
                return resid[:, t, c * P:(c + 1) * P]

            def o_chunk(t, c):
                at = c * P if c < AW // P else QH + c * P - AW
                return z[:, t, at:at + P]

            def ffn(n0, b0, u_x, u_h, f):
                even, odd = acc[b0 % 2], acc[(b0 + 1) % 2]

                def turn_hidden(i):
                    pe.wait_ge(hidden_ready, f * FB + i)
                    pe.wait_ge(turn_rest, u_h - BPB + BPB * i)
                    turn_chunks(lambda t, c: hidden[:, t, c * P:(c + 1) * P], turn[0:BPB])

                def gate(i, peeled):
                    for s in range(KS):
                        if peeled:
                            pe.wait_ge(turn_rest, u_x + s + 1)
                        use_slot(n0 + s + 2 * KS * i, s % RING, x_high, x_rest, CPS * s, even, s == 0, s == KS - 1)
                        if s == 1 and not peeled:
                            turn_hidden(i)

                def up(i):
                    for s in range(KS):
                        use_slot(n0 + KS + s + 2 * KS * i, s % RING, x_high, x_rest, CPS * s, odd, s == 0, s == KS - 1)

                if f:
                    pe.wait_ge(branch_ready, CREDIT + 2 * NBD - 1)
                else:
                    pe.wait_ge(gain_T_ready, 1)
                gate(0, True)
                if f:
                    pe.wait_ge(branch_ready, CREDIT + 2 * NBD)
                up(0)
                with pe.Fori(1, FB) as i:
                    pe.wait_ge(silu_ready, f * FB + i)
                    gate(i, False)
                    pe.wait_ge(hidden_ready, f * FB + i)
                    up(i)
                turn_hidden(FB)

            def down(n0, b0, u_h, f):
                pe.wait_ge(silu_ready, f * FB + FB)
                with pe.Fori(0, NBD // 2) as j:
                    for h in range(2):
                        pe.wait_ge(branch_ready, CREDIT - 1 + 2 * NBD * f + 2 * j + h)
                        for s in range(FS):
                            pe.wait_ge(turn_rest, u_h + s + 1)
                            use_slot(n0 + FS * h + s + 2 * FS * j, (FS * h + s) % RING, h_high, h_rest, CPS * s,
                                     acc[(b0 + h) % 2], s == 0, s == FS - 1)

            def over_x(n0, b0, blocks, u_x, moved, before):
                with pe.Fori(0, blocks // 2) as j:
                    for h in range(2):
                        pe.wait_ge(moved, CREDIT - 1 + before + 2 * j + h)
                        for s in range(KS):
                            pe.wait_ge(turn_rest, u_x + s + 1)
                            use_slot(n0 + KS * h + s + 2 * KS * j, s % RING, x_high, x_rest, CPS * s,
                                     acc[(b0 + h) % 2], s == 0, s == KS - 1)

            pe.wait_ge(gains_landed, 16 * (NG + 1))
            pe.wait_ge(ident_ready, 1)
            nc.tensor.transpose(bank[0][:, 0:NG * KC], gain_in[0:NG * KC, :], ident[0:NG * KC, 0:NG * KC]
                                ).then_inc(gain_turned, 1)
            for nb in range(NBD):
                turn_block(resid_chunk, U_X1, nb, x_landed[nb], 16)
            ffn(S_FFN1, 0, U_X1, U_H1, 0)
            down(S_DOWN1, 2 * FB, U_H1, 0)
            for nb in range(NBD):
                turn_block(resid_chunk, U_MIX, nb, resid_ready, R_MIX + nb + 1)
            over_x(S_QKV, B_QKV, QB, U_MIX, z_ready, 0)
            pe.wait_ge(z_ready, CREDIT + QB - 1)
            for s in range(KS):
                use_slot(S_TAIL + s, s % RING, x_high, x_rest, CPS * s, acc[B_TAIL % 2], s == 0, s == KS - 1, TAIL)
            pe.wait_ge(count_ready, 1)
            pe.wait_ge(z_ready, CREDIT + QB)
            for c in range(3):
                ins = nc.tensor.transpose(bank[2][:, c * P:(c + 1) * P], count[:, c * P:(c + 1) * P], ident[:])
            ins.then_inc(count_turned, 1)

            def turn_pair(pr):
                if pr:
                    pe.wait_ge(q_T_ready, pr)
                at = pr * P if pr < PAIRS_A else QH + (pr - PAIRS_A) * P
                for t in range(T):
                    ins = nc.tensor.transpose(bank[4][:, t * P:(t + 1) * P], z[:, t, at:at + P], ident[:])
                if pr and pr <= PAIRS_A:
                    pe.wait_ge(k_T_ready, pr)
                if pr < PAIRS_A:
                    for t in range(T):
                        ins = nc.tensor.transpose(bank[5][:, t * P:(t + 1) * P],
                                                  z[:, t, AW + at:AW + at + P], ident[:])
                if pr == PAIRS_A:
                    pe.wait_ge(vals_ready, T + 3 * T)
                    for t in range(T):
                        nc.tensor.transpose(bank[5][:, t * P:(t + 1) * P], z[:, t, KB:KB + P], ident[:])
                    for t in range(T):
                        ins = nc.tensor.transpose(bank[5][:, S + t * P:S + (t + 1) * P], k_swap[:, t, :], ident[:])
                ins.then_inc(pair_turned, 1)

            def keys(h):
                lo = HD * (h % 2)
                if h < AH:
                    return qk_T[lo:lo + HD, (h // 2) % 2, 1, :]
                return kb_T[lo:lo + HD, ((h - AH) // (BH // KVH) + h) % 2, :]

            turn_pair(0)
            for g in range(H + 2):
                if g < H:
                    if g % 2 == 0 and g // 2 + 1 < PAIRS:
                        if g // 2 + 1 == PAIRS_A:
                            pe.wait_ge(z_ready, CREDIT + QB + 1)
                        turn_pair(g // 2 + 1)
                    pe.wait_ge(q_T_ready, g // 2 + 1)
                    pe.wait_ge(k_T_ready, min(g // 2, PAIRS_A) + 1)
                    if g >= 2:
                        pe.wait_ge(scores_read, g - 1)
                    lo = HD * (g % 2)
                    q = qk_T[lo:lo + HD, (g // 2) % 2, 0, :]
                    nc.tensor.matmul(bank[g % 2][:, 0:S], q[:, P:S], keys(g), start=True, stop=True)
                    nc.tensor.matmul(bank[g % 2][:, S:S + P], q[:, 0:P], keys(g)[:, 0:P], start=True, stop=True
                                     ).then_inc(scored, 1)
                if 1 <= g <= H:
                    h = g - 1
                    pe.wait_ge(prob_ready, h + 1)
                    if h >= 2:
                        wait_prob_T(pe, h - 2)
                    else:
                        pe.wait_ge(count_T_ready, 1)
                    for c in range(3):
                        ins = nc.tensor.transpose(bank[2 + h % 2][:, c * P:(c + 1) * P],
                                                  prob[:, h % 2, c * P:(c + 1) * P], ident[:])
                    ins.then_inc(prob_turned, 1)
                if g >= 2:
                    h = g - 2
                    wait_prob_T(pe, h)
                    if h == 0:
                        pe.wait_ge(vals_ready, T)
                    if h % GROUP == 0 and h:
                        pe.wait_ge(o_ready, h // GROUP)
                    v = h if h < AH else AH + (h - AH) // (BH // KVH)
                    w = prob_T[:, h % 2, :]
                    o = [bank[6 + t][:, (h % GROUP) * P:(h % GROUP) * P + VW] for t in range(T)]
                    nc.tensor.matmul(o[1], w[:, 0:P], vals[:, 0, v, :], start=True, stop=False)
                    nc.tensor.matmul(o[1], w[:, P:2 * P], vals[:, 1, v, :], start=False, stop=True)
                    nc.tensor.matmul(o[0], w[:, 2 * P:3 * P], vals[:, 0, v, :], start=True, stop=True
                                     ).then_inc(weighed, 1)
            for nb in range(NBD):
                turn_block(o_chunk, U_O, nb, resid_ready, R_O + nb + 1)
            over_x(S_WO, B_WO, NBD, U_O, branch_ready, NBD)
            for nb in range(NBD):
                turn_block(resid_chunk, U_X2, nb, resid_ready, R_X2 + nb + 1)
            ffn(S_FFN2, B_FFN2, U_X2, U_H2, 1)
            down(S_DOWN2, B_FFN2 + 2 * FB, U_H2, 1)
            pe.wait_ge(p_landed, 16)
            for c in range(PC):
                for t in range(T):
                    ins = nc.tensor.transpose(turn[0][:, (c * T + t) * P:(c * T + t + 1) * P],
                                              p_sb[:, t, c * P:(c + 1) * P], ident[:])
            ins.then_inc(turned, 1)
            for nb in range(NBD):
                if nb < 2:
                    pe.wait_ge(branch_ready, CREDIT + 3 * NBD - 1 + nb)
                else:
                    pe.wait_ge(emb_ready, nb - 1)
                pe.wait_ge(turn_rest, U_PLE)
                use_slot(S_PROJ + nb, nb, p_high, p_rest, 0, acc[(B_PROJ + nb) % 2], True, True)
                if nb:
                    turn_block(resid_chunk, U_PLE, nb - 1, resid_ready, R_PLE + nb)
            turn_block(resid_chunk, U_PLE, NBD - 1, resid_ready, R_PLE + NBD)
            pe.wait_ge(emb_ready, NBD)
            over_x(S_GATE, B_GATE, NBD, U_PLE, sig_ready, 0)

        @block.scalar
        def _(act):
            def high(n, k, width=NB):
                if isinstance(n, int) and n >= S_END:
                    return
                act.wait_ge(w_landed[k], 4 * n - 4 * k + 16)
                if not (isinstance(n, int) and n < RING):
                    act.wait_ge(w_used, n - (RING - 1))
                nc.scalar.copy(w_high[:, k, :, 0:width], raw[:, k, :, 0:width]).then_inc(w_high_done, 1)

            def ahead(n, s0, count_, k0=0):
                for s in range(s0, s0 + count_):
                    high(n + s + RING, (k0 + s) % RING)

            def square(q, src, job, t, b):
                if not (isinstance(q, int) and q < 2):
                    act.wait_ge(squared, q - 1)
                nc.scalar.activation(junk[:, t % 2, :], src, ACT.Square, accum_out=stat[:, job, t, b]
                                     ).then_inc(squared, 1)

            def col(b):
                return slice(b, b + 1)

            def blk(b):
                return slice(b * NB, (b + 1) * NB)

            def x_block(u, nb, gain):
                for j in range(BPB):
                    act.wait_ge(turned, u + BPB * nb + j + 1)
                    for c in range(CPS):
                        ch = nb * CB + CPS * j + c
                        ins = nc.scalar.activation(x_high[:, ch, :], turn[BPB * (nb % 2) + j][:, c * S:(c + 1) * S],
                                                   ACT.Copy, scale=gain_T[:, gain + ch:gain + ch + 1])
                    ins.then_inc(turn_high, 1)

            def resid_block(u, nb, gain, job):
                x_block(u, nb, gain)
                for t in range(T):
                    square(Q[job] + T * nb + t, resid[:, t, blk(nb)], job, t, col(nb))

            def ffn(n0, b0, u_h, job):
                def silu(i):
                    act.wait_ge(w_used, n0 + KS + 2 * KS * i)
                    for t in range(T):
                        ins = nc.scalar.activation(silu_g[:, t, :], acc[b0 % 2][t][:], ACT.Silu,
                                                   scale=rstd[:, job, t:t + 1])
                    ins.then_inc(silu_ready, 1)

                def hidden_high(i):
                    for j in range(BPB):
                        act.wait_ge(turned, u_h - BPB + j + 1 + BPB * i)
                        nc.scalar.copy(h_high[:, bass.ds(CB * i - CB + CPS * j, CPS), :],
                                       turn[j][:].rearrange("p (c s) -> p c s", c=CPS)).then_inc(turn_high, 1)

                ahead(n0, 0, KS - 1)
                act.wait_ge(rstd_ready, job + 1)
                silu(0)
                ahead(n0, KS - 1, KS + 1)
                with act.Fori(1, FB) as i:
                    n = n0 + 2 * KS * i
                    ahead(n, 0, 3)
                    hidden_high(i)
                    ahead(n, 3, KS - 4)
                    silu(i)
                    ahead(n, KS - 1, KS + 1)
                hidden_high(FB)

            def down(n0, b0, job):
                with act.Fori(0, NBD // 2) as j:
                    for h in range(2):
                        n = n0 + FS * h + 2 * FS * j
                        ahead(n, 0, FS - 1, FS * h)
                        act.wait_ge(w_used, n + FS)
                        for t in range(T):
                            square(Q[job] + T * h + t + 2 * T * j, acc[(b0 + h) % 2][t][:], job, t,
                                   bass.ds(2 * j + h, 1))
                        ahead(n, FS - 1, 1, FS * h)

            for n, g in enumerate((g_ffn1_pre, g_mix_pre, None, g_ffn2_pre, g_ple_pre)):
                for src, at in [(g_out_a, 0), (g_out_b, AW // P)] if g is None else [(g, 0)]:
                    v = src[0].rearrange("(c p) -> c p", p=P)
                    act.dma_start(gain_in[n * KC + at:n * KC + at + v.shape[0], :], v).then_inc(gains_landed, 16)
            act.dma_start(sinks[:], attn_sinks.rearrange("a k g -> a (k g)").to_broadcast([P, BH])
                          ).then_inc(sinks_landed, 16)
            act.wait_ge(ident_ready, 1)
            nc.scalar.copy(spare[:, 2:3], ident[:, 0:1]).then_inc(sig_ready, CREDIT)
            for k in range(RING):
                high(k, k)
            act.wait_ge(gain_T_ready, 1)
            for nb in range(NBD):
                resid_block(U_X1, nb, G_FFN1, J_IN1)
            ffn(S_FFN1, 0, U_H1, J_IN1)
            down(S_DOWN1, 2 * FB, J_POST1)
            for nb in range(NBD):
                resid_block(U_MIX, nb, G_MIX, J_MIX)
            with act.Fori(0, QB // 2 - 1) as j:
                ahead(S_QKV + 2 * KS * j, 0, 2 * KS)
            for n in range(S_TAIL - 2 * KS, S_WO):
                high(n + RING, n % RING, tail_or_block(n + RING))

            def keys_out(pr):
                act.wait_ge(pair_turned, pr + 1)
                if pr < PAIRS_A:
                    if pr >= 2:
                        act.wait_ge(scored, 2 * pr - 2)
                    nc.scalar.copy(qk_T[:, pr % 2, 1, :], bank[5][:, 0:S]).then_inc(k_T_ready, 1)
                else:
                    nc.scalar.copy(kb_T[:].rearrange("p a s -> p (a s)"), bank[5][:]).then_inc(k_T_ready, 1)

            act.wait_ge(sinks_landed, 16)
            keys_out(0)
            for g in range(H + 1):
                if g < H:
                    if g % 2 == 0 and g // 2 + 1 <= PAIRS_A:
                        keys_out(g // 2 + 1)
                    act.wait_ge(peak_ready, g + 1)
                    if g >= 2:
                        act.wait_ge(prob_turned, g - 1)
                    nc.scalar.activation(prob[:, g % 2, 0:S], score[:, g % 2, 0:S], ACT.Exp,
                                         bias=neg_peak[:, g % 2, 1:2])
                    if g >= AH:
                        nc.scalar.activation(sink_e[:, g - AH, :], neg_peak[:, g % 2, :], ACT.Exp,
                                             bias=sinks[:, g - AH:g - AH + 1])
                    nc.scalar.activation(prob[:, g % 2, S:S + P], score[:, g % 2, S:S + P], ACT.Exp,
                                         bias=neg_peak[:, g % 2, 0:1]).then_inc(prob_ready, 1)
                if g > AH:
                    h = g - 1
                    act.wait_ge(prob_turned, h + 1)
                    act.wait_ge(weighed, h - 1)
                    nc.scalar.copy(prob_T[:, h % 2, :], bank[2 + h % 2][:, 0:3 * P]).then_inc(prob_T_b, 1)
            act.wait_ge(o_ready, H // GROUP)
            for job, at in ((J_OA, 0), (J_OB, QH)):
                for b in range(OBLK):
                    for t in range(T):
                        square(Q[job] + T * b + t, z[:, t, at + b * NB:at + (b + 1) * NB], job, t, col(b))
            for nb in range(NBD):
                x_block(U_O, nb, G_O)
            with act.Fori(0, NBD // 2) as j:
                for h in range(2):
                    n = S_WO + KS * h + 2 * KS * j
                    ahead(n, 0, KS - 1)
                    for t in range(T):
                        act.wait_ge(biased, 2 * T * j + T * h + t + 1)
                        square(Q[J_POSTM] + T * h + t + 2 * T * j, branch[:, t, bass.ds(2 * NB * j + NB * h, NB)],
                               J_POSTM, t, bass.ds(2 * j + h, 1))
                    ahead(n, KS - 1, 1)
            for nb in range(NBD):
                resid_block(U_X2, nb, G_FFN2, J_IN2)
            ffn(S_FFN2, B_FFN2, U_H2, J_IN2)
            down(S_DOWN2, B_FFN2 + 2 * FB, J_POST2)
            act.wait_ge(turned, U_P + 1)
            nc.scalar.copy(p_high[:].rearrange("p c s -> p (c s)"), turn[0][:]).then_inc(turn_high, 1)
            act.dma_start(ple_row[:], g_ple_post[:, :].to_broadcast([P, D])).then_inc(ple_row_landed, 16)
            for nb in range(NBD):
                act.wait_ge(w_used, S_PROJ + nb + 1)
                for t in range(T):
                    ins = nc.scalar.copy(emb[:, t, blk(nb)], acc[(B_PROJ + nb) % 2][t][:])
                ins.then_inc(emb_ready, 1)
                high(S_PROJ + nb + RING, nb)
                if nb:
                    resid_block(U_PLE, nb - 1, G_PLE, J_PLE)
            resid_block(U_PLE, NBD - 1, G_PLE, J_PLE)
            for nb in range(NBD):
                n = S_GATE + KS * nb
                ahead(n, 0, KS - 1)
                act.wait_ge(rstd_ready, J_PLE + 1)
                act.wait_ge(w_used, n + KS)
                if nb:
                    act.wait_ge(gated_ready, T * nb)
                for t in range(T):
                    ins = nc.scalar.activation(sig[:, t, :], acc[(B_GATE + nb) % 2][t][:], ACT.Sigmoid,
                                               scale=rstd[:, J_PLE, t:t + 1])
                ins.then_inc(sig_ready, 1)
                ahead(n, KS - 1, 1)
                for t in range(T):
                    act.wait_ge(gated_ready, T * nb + t + 1)
                    square(Q[J_POSTP] + T * nb + t, gated[:, t, :], J_POSTP, t, col(nb))

        @block.vector
        def _(dve):
            steps = [0]

            def step(ins):
                steps[0] += 1
                ins.then_inc(dve_step, 1)
                dve.wait_ge(dve_step, steps[0])

            def rest(n, k, width=NB):
                if isinstance(n, int) and n >= S_END:
                    return
                dve.wait_ge(w_high_done, n + 1)
                nc.vector.tensor_tensor(w_rest[:, k, :, 0:width], raw[:, k, :, 0:width],
                                        w_high[:, k, :, 0:width].bitcast(F32), ALU.subtract).then_inc(w_rest_done, 1)

            def ahead(n, s0, count_, k0=0):
                for s in range(s0, s0 + count_):
                    rest(n + s + RING, (k0 + s) % RING)

            def blk(b):
                return slice(b * NB, (b + 1) * NB)

            def reduce(job):
                dve.wait_ge(squared, Q[job + 1])
                nc.vector.reduce_sum(ssum[:, job, :], stat[:, job, :, 0:squares[job] // T], axis=AX.X
                                     ).then_inc(summed, 1)

            def x_rest_block(u, nb, gain):
                for j in range(BPB):
                    dve.wait_ge(turn_high, u + BPB * nb + j + 1)
                    for c in range(CPS):
                        ch = nb * CB + CPS * j + c
                        ins = nc.vector.scalar_tensor_tensor(
                            out=x_rest[:, ch, :], in0=turn[BPB * (nb % 2) + j][:, c * S:(c + 1) * S],
                            scalar=gain_T[:, gain + ch:gain + ch + 1], in1=x_high[:, ch, :].bitcast(F32),
                            op0=ALU.mult, op1=ALU.subtract)
                    ins.then_inc(turn_rest, 1)

            def add_branch(job):
                def update(nb):
                    for t in range(T):
                        ins = nc.vector.scalar_tensor_tensor(out=resid[:, t, blk(nb)], in0=branch[:, t, blk(nb)],
                                                             scalar=rstd[:, job, t:t + 1], in1=resid[:, t, blk(nb)],
                                                             op0=ALU.mult, op1=ALU.add)
                    ins.then_inc(resid_ready, 1)
                return update

            def boundary(u, gain, update):
                update(0)
                for nb in range(NBD):
                    if nb + 1 < NBD:
                        update(nb + 1)
                    x_rest_block(u, nb, gain)

            def ffn(n0, b0, u_h, job, f):
                def gate_up(i):
                    dve.wait_ge(w_used, n0 + 2 * KS + 2 * KS * i)
                    dve.wait_ge(silu_ready, f * FB + 1 + i)
                    for t in range(T):
                        ins = nc.vector.scalar_tensor_tensor(out=hidden[:, t, :], in0=acc[(b0 + 1) % 2][t][:],
                                                             scalar=rstd[:, job, t:t + 1], in1=silu_g[:, t, :],
                                                             op0=ALU.mult, op1=ALU.mult)
                    ins.then_inc(hidden_ready, 1)

                def hidden_rest(i):
                    for j in range(BPB):
                        chunks = bass.ds(CB * i - CB + CPS * j, CPS)
                        dve.wait_ge(turn_high, u_h - BPB + j + 1 + BPB * i)
                        nc.vector.tensor_tensor(h_rest[:, chunks, :], turn[j][:].rearrange("p (c s) -> p c s", c=CPS),
                                                h_high[:, chunks, :].bitcast(F32), ALU.subtract).then_inc(turn_rest, 1)

                ahead(n0, 0, 2 * KS - 1)
                dve.wait_ge(rstd_ready, job + 1)
                gate_up(0)
                ahead(n0, 2 * KS - 1, 1)
                with dve.Fori(1, FB) as i:
                    n = n0 + 2 * KS * i
                    ahead(n, 0, 3)
                    hidden_rest(i)
                    ahead(n, 3, 2 * KS - 4)
                    gate_up(i)
                    ahead(n, 2 * KS - 1, 1)
                hidden_rest(FB)

            def down(n0, b0, job, f):
                with dve.Fori(0, NBD // 2) as j:
                    for h in range(2):
                        n = n0 + FS * h + 2 * FS * j
                        ahead(n, 0, FS - 1, FS * h)
                        dve.wait_ge(row_landed[h], 32 * f + 16 + 16 * j)
                        for t in range(T):
                            dve.wait_ge(squared, Q[job] + T * h + t + 1 + 2 * T * j)
                            ins = nc.vector.tensor_tensor(branch[:, t, bass.ds(2 * NB * j + NB * h, NB)],
                                                          acc[(b0 + h) % 2][t][:], gain_row[:, h, :], ALU.mult)
                        ins.then_inc(branch_ready, 1)
                        ahead(n, FS - 1, 1, FS * h)

            def take_branch(job, blocks):
                reduce(job)
                dve.wait_ge(branch_ready, CREDIT + blocks)
                dve.wait_ge(rstd_ready, job + 1)

            nc.vector.memset(spare[:, 0:1], 0.0).then_inc(branch_ready, CREDIT)
            nc.vector.memset(spare[:, 1:2], 0.0).then_inc(z_ready, CREDIT)
            dve.wait_ge(gain_turned, 1)
            nc.vector.tensor_copy(gain_T[:], bank[0][:, 0:NG * KC]).then_inc(gain_T_ready, 1)
            dve.wait_ge(gain_T_ready, 1)
            for k in range(RING):
                rest(k, k)
            for nb in range(NBD):
                x_rest_block(U_X1, nb, G_FFN1)
            reduce(J_IN1)
            ffn(S_FFN1, 0, U_H1, J_IN1, 0)
            down(S_DOWN1, 2 * FB, J_POST1, 0)
            take_branch(J_POST1, NBD)
            boundary(U_MIX, G_MIX, add_branch(J_POST1))
            reduce(J_MIX)

            def project_out(j, h):
                dve.wait_ge(w_used, S_QKV + KS * (h + 1) + 2 * KS * j)
                at = bass.ds(2 * NB * j + NB * h, NB)
                for t in range(T):
                    ins = nc.vector.scalar_tensor_tensor(out=z[:, t, at], in0=acc[(B_QKV + h) % 2][t][:],
                                                         scalar=rstd[:, J_MIX, t:t + 1], in1=bias_row[:, at],
                                                         op0=ALU.mult, op1=ALU.add)
                ins.then_inc(z_ready, 1)

            dve.wait_ge(rstd_ready, J_MIX + 1)
            dve.wait_ge(bias_landed, 16)
            with dve.Fori(0, QB // 2 - 1) as j:
                for h in range(2):
                    n = S_QKV + KS * h + 2 * KS * j
                    ahead(n, 0, KS - 1)
                    project_out(j, h)
                    ahead(n, KS - 1, 1)

            dve.wait_ge(dist_ready, 2)
            step(nc.vector.tensor_copy(tmp[:], dist_i[:]))
            step(nc.vector.tensor_scalar(count[:], tmp[:], float(P), None, ALU.is_le))
            for dil in (4, 16):
                step(nc.vector.tensor_scalar(bits[:], dist_i[:], dil - 1, None, ALU.bitwise_and))
                step(nc.vector.tensor_copy(dist_a[:], bits[:]))
                step(nc.vector.scalar_tensor_tensor(out=count[:], in0=dist_a[:], scalar=0.0, in1=count[:],
                                                    op0=ALU.is_equal, op1=ALU.add))
            nc.vector.scalar_tensor_tensor(out=count[:], in0=tmp[:], scalar=0.0, in1=count[:],
                                           op0=ALU.is_ge, op1=ALU.mult).then_inc(count_ready, 1)
            dve.wait_ge(count_ready, 1)
            step(nc.vector.tensor_scalar(dist_b[:], count[:], 0.0, BIG, ALU.is_equal, ALU.mult))
            step(nc.vector.tensor_tensor(dist_a[:], dist_b[:], tmp[:], ALU.add))
            step(nc.vector.tensor_scalar(dist_b[:], tmp[:], 0.0, BIG, ALU.is_lt, ALU.mult))
            step(nc.vector.tensor_tensor(dist_b[:], dist_b[:], tmp[:], ALU.add))
            step(nc.vector.tensor_scalar(tmp[:], tmp[:], float(P), BIG, ALU.is_ge, ALU.mult))
            step(nc.vector.tensor_tensor(dist_b[:], dist_b[:], tmp[:], ALU.add))

            for b in range(QB - 2, QB):
                n = S_QKV + KS * b
                for s in range(KS):
                    if s == KS - 1:
                        project_out(QB // 2 - 1, b - (QB - 2))
                    rest(n + s + RING, s % RING, tail_or_block(n + s + RING))
            for s in range(KS):
                if s == KS - 1:
                    dve.wait_ge(w_used, S_TAIL + KS)
                    for t in range(T):
                        ins = nc.vector.scalar_tensor_tensor(
                            out=z[:, t, QB * NB:QKV], in0=acc[B_TAIL % 2][t][:, 0:TAIL],
                            scalar=rstd[:, J_MIX, t:t + 1], in1=bias_row[:, QB * NB:QKV],
                            op0=ALU.mult, op1=ALU.add)
                    ins.then_inc(z_ready, 1)
                rest(S_TAIL + s + RING, s % RING, tail_or_block(S_TAIL + s + RING))

            def queries_out(pr):
                dve.wait_ge(pair_turned, pr + 1)
                if pr >= 2:
                    dve.wait_ge(scored, 2 * pr - 2)
                nc.vector.tensor_scalar(qk_T[:, pr % 2, 0, :], bank[4][:, 0:S], HD ** -0.5, None, ALU.mult
                                        ).then_inc(q_T_ready, 1)

            def group_out(q):
                dve.wait_ge(weighed, GROUP * (q + 1))
                at = q * GROUP * HD
                if q * GROUP >= AH:
                    at += QH - AW
                for t in range(T):
                    o = bank[6 + t][:].rearrange("p (h c) -> p h c", h=GROUP)
                    if q * GROUP < AH:
                        step(nc.vector.reciprocal(denom[:, t, :], o[:, :, HD]))
                    else:
                        h0 = q * GROUP - AH
                        step(nc.vector.tensor_tensor(denom[:, t, :], o[:, :, HD], sink_e[:, h0:h0 + GROUP, t], ALU.add))
                        step(nc.vector.reciprocal(denom[:, t, :], denom[:, t, :]))
                    ins = nc.vector.tensor_tensor(
                        z[:, t, at:at + GROUP * HD].rearrange("p (h d) -> p h d", d=HD), o[:, :, 0:HD],
                        denom[:, t, :].unsqueeze(2).to_broadcast([P, GROUP, HD]), ALU.mult)
                ins.then_inc(o_ready, 1)

            dve.wait_ge(count_turned, 1)
            nc.vector.tensor_copy(count_T[:], bank[2][:, 0:3 * P]).then_inc(count_T_ready, 1)
            dve.wait_ge(count_T_ready, 1)
            queries_out(0)
            for g in range(H + 3):
                if g < H:
                    if g % 2 == 0 and g // 2 + 1 < PAIRS:
                        queries_out(g // 2 + 1)
                    dve.wait_ge(scored, g + 1)
                    if g >= 2:
                        dve.wait_ge(prob_ready, g - 1)
                    nc.vector.scalar_tensor_tensor(out=score[:, g % 2, :], in0=(dist_a if g < AH else dist_b)[:],
                                                   scalar=-head_slope[g], in1=bank[g % 2][:, 0:3 * P],
                                                   op0=ALU.mult, op1=ALU.add).then_inc(scores_read, 1)
                if 1 <= g <= AH:
                    h = g - 1
                    dve.wait_ge(prob_turned, h + 1)
                    if h >= 2:
                        dve.wait_ge(weighed, h - 1)
                    nc.vector.tensor_tensor(prob_T[:, h % 2, :], bank[2 + h % 2][:, 0:3 * P], count_T[:], ALU.mult
                                            ).then_inc(prob_T_a, 1)
                if g < H:
                    dve.wait_ge(scores_read, g + 1)
                    nc.vector.reduce_max(peak[:, g % 2, 1:2], score[:, g % 2, 0:S], axis=AX.X)
                    nc.vector.reduce_max(peak[:, g % 2, 0:1], score[:, g % 2, S:S + P], axis=AX.X
                                         ).then_inc(peak_found, 1)
                if g >= 6 and (g - 6) % GROUP == 0:
                    group_out((g - 6) // GROUP)
                if g < H:
                    dve.wait_ge(peak_found, g + 1)
                    if g < AH:
                        ins = nc.vector.tensor_scalar(neg_peak[:, g % 2, :], peak[:, g % 2, :], -1.0, None, ALU.mult)
                    else:
                        ins = nc.vector.tensor_scalar(neg_peak[:, g % 2, :], peak[:, g % 2, :],
                                                      sinks[:, g - AH:g - AH + 1], -1.0, ALU.max, ALU.mult)
                    ins.then_inc(peak_ready, 1)
            reduce(J_OA)
            reduce(J_OB)
            dve.wait_ge(rstd_ready, J_OB + 1)
            dve.wait_ge(o_ready, H // GROUP)

            def scale_o(nb):
                job = J_OA if nb < OBLK else J_OB
                at = nb * NB if nb < OBLK else QH - AW + nb * NB
                for t in range(T):
                    ins = nc.vector.tensor_scalar(z[:, t, at:at + NB], z[:, t, at:at + NB], rstd[:, job, t:t + 1],
                                                  None, ALU.mult)
                ins.then_inc(resid_ready, 1)

            boundary(U_O, G_O, scale_o)
            dve.wait_ge(mix_rows_landed, 32)
            with dve.Fori(0, NBD // 2) as j:
                for h in range(2):
                    n = S_WO + KS * h + 2 * KS * j
                    at = bass.ds(2 * NB * j + NB * h, NB)
                    ahead(n, 0, KS - 1)
                    dve.wait_ge(w_used, n + KS)
                    for t in range(T):
                        nc.vector.tensor_tensor(branch[:, t, at], acc[(B_WO + h) % 2][t][:], bias_row[:, at], ALU.add
                                                ).then_inc(biased, 1)
                    for t in range(T):
                        dve.wait_ge(squared, Q[J_POSTM] + T * h + t + 1 + 2 * T * j)
                        ins = nc.vector.tensor_tensor(branch[:, t, at], branch[:, t, at],
                                                      bias_row[:, bass.ds(2 * NB * j + NB * h + D, NB)], ALU.mult)
                    ins.then_inc(branch_ready, 1)
                    ahead(n, KS - 1, 1)
            take_branch(J_POSTM, 2 * NBD)
            boundary(U_X2, G_FFN2, add_branch(J_POSTM))
            reduce(J_IN2)
            ffn(S_FFN2, B_FFN2, U_H2, J_IN2, 1)
            down(S_DOWN2, B_FFN2 + 2 * FB, J_POST2, 1)
            reduce(J_POST2)
            dve.wait_ge(turn_high, U_P + 1)
            nc.vector.tensor_tensor(p_rest[:].rearrange("p c s -> p (c s)"), turn[0][:],
                                    p_high[:].rearrange("p c s -> p (c s)").bitcast(F32), ALU.subtract
                                    ).then_inc(turn_rest, 1)
            dve.wait_ge(branch_ready, CREDIT + 3 * NBD)
            dve.wait_ge(rstd_ready, J_POST2 + 1)
            update = add_branch(J_POST2)
            for nb in range(NBD):
                update(nb)
                rest(S_PROJ + nb + RING, nb)
                if nb:
                    x_rest_block(U_PLE, nb - 1, G_PLE)
            x_rest_block(U_PLE, NBD - 1, G_PLE)
            reduce(J_PLE)
            dve.wait_ge(ple_row_landed, 16)
            for nb in range(NBD):
                n = S_GATE + KS * nb
                ahead(n, 0, KS - 1)
                dve.wait_ge(sig_ready, CREDIT + nb + 1)
                if nb:
                    dve.wait_ge(squared, Q[J_POSTP] + T * nb)
                for t in range(T):
                    nc.vector.tensor_tensor(gated[:, t, :], sig[:, t, :], emb[:, t, blk(nb)], ALU.mult
                                            ).then_inc(gated_ready, 1)
                for t in range(T):
                    dve.wait_ge(gated_ready, T * nb + t + 1)
                    ins = nc.vector.tensor_tensor(branch[:, t, blk(nb)], gated[:, t, :], ple_row[:, blk(nb)], ALU.mult)
                ins.then_inc(branch_ready, 1)
                ahead(n, KS - 1, 1)
            take_branch(J_POSTP, 4 * NBD)
            update = add_branch(J_POSTP)
            for nb in range(NBD):
                update(nb)


_OUT = (1, 256, 2048)


def kernel(**inputs):
    import numpy as _np
    import concourse.bacc as _bacc
    from concourse.bass_utils import run_bass_kernel_spmd as _run

    nc = _bacc.Bacc("TRN2", target_bir_lowering=False, num_devices=1)
    arrays, args = {}, {}
    for name, value in inputs.items():
        a = _np.ascontiguousarray(value)
        arrays[f"in_{name}"] = a
        args[name] = nc.dram_tensor(f"in_{name}", a.shape, mybir.dt.from_np(a.dtype), kind="ExternalInput").ap()
    out = nc.dram_tensor("out_h", _OUT, F32, kind="ExternalOutput").ap()
    layer_program(nc, out=out, **args)
    r = _run(nc, [arrays], core_ids=[0])
    return r.results[0]["out_h"]
```

```python
from contextlib import ExitStack

import concourse.bass as bass
from concourse import mybir

F32 = mybir.dt.float32
F32R = mybir.dt.float32r
BF16 = mybir.dt.bfloat16
I32 = mybir.dt.int32
ALU = mybir.AluOpType
ACT = mybir.ActivationFunctionType
AX = mybir.AxisListType

P = 128
NB = 512
RING = 4
CPS = 2
EPS = 1e-6
HD = 64
BIG = 1e30
VW = HD + 2


def layer_program(nc, x, p, g_ffn1_pre, w_ffn1_gate, w_ffn1_up, w_ffn1_down, g_ffn1_post,
                  g_mix_pre, w_qkv, b_qkv, attn_sinks, g_out_a, g_out_b, w_o, b_o, g_mix_post,
                  g_ffn2_pre, w_ffn2_gate, w_ffn2_up, w_ffn2_down, g_ffn2_post,
                  g_ple_pre, w_ple_gate, w_ple_proj, g_ple_post, out):
    _, S, D = x.shape
    F = w_ffn1_gate.shape[2]
    QKV = w_qkv.shape[2]
    PLE = p.shape[3]
    AW = g_out_a.shape[1]
    AH = AW // HD
    BH = attn_sinks.shape[1] * attn_sinks.shape[2]
    KVH = attn_sinks.shape[1]
    H = AH + BH
    T = S // P
    KC = D // P
    FC = F // P
    NBD = D // NB
    FB = F // NB
    CB = NB // P
    KS, FS = KC // CPS, FC // CPS
    QB, TAIL = QKV // NB, QKV % NB
    PC = PLE // P
    assert T == 2 and PC == CPS and KVH == 2 and CB == 4 and KS % RING == 0 and 2 * FS % RING == 0
    slope = [2.0 ** (-8.0 * (n + 1) / H) for n in range(H)]
    head_slope = slope[1::2] + slope[0::2]

    S_FFN1 = 0
    S_DOWN1 = S_FFN1 + 2 * KS * FB
    S_QKV = S_DOWN1 + NBD * FS
    S_WO = S_QKV + (QB + 1) * KS
    S_FFN2 = S_WO + NBD * KS
    S_DOWN2 = S_FFN2 + 2 * KS * FB
    S_PROJ = S_DOWN2 + NBD * FS
    S_GATE = S_PROJ + NBD
    S_END = S_GATE + NBD * KS
    QH = 3 * AW
    KB = QH + BH * HD
    VB = KB + KVH * HD
    ZK, ZQ, ZKB = AW, 2 * AW, 2 * AW + BH * HD
    ZW = ZKB + KVH * HD
    QKV_BLOCKS = [(QH, NB), (KB, TAIL), (QH + NB, NB)] + [(part * AW + half * NB, NB)
                                                          for half in range(AW // NB) for part in range(3)]
    assert len(QKV_BLOCKS) == QB + 1 and sum(w for _, w in QKV_BLOCKS) == QKV
    B_QKV = 2 * FB + NBD
    B_WO = B_QKV + QB + 1
    B_FFN2 = B_WO + NBD
    B_PROJ = B_FFN2 + 2 * FB + NBD
    B_GATE = B_PROJ + NBD
    BPB = CB // CPS
    XU = KC // CPS
    U_X1 = 0
    U_H1 = U_X1 + XU
    U_MIX = U_H1 + BPB * FB
    U_O = U_MIX + XU
    U_X2 = U_O + XU
    U_H2 = U_X2 + XU
    U_P = U_H2 + BPB * FB
    U_PLE = U_P + 1
    UW = NB // BPB
    O_UNITS = list(range(XU // 2, XU)) + list(range(XU // 2))
    X_UNITS = list(range(XU))
    J_IN1, J_POST1, J_MIX, J_OB, J_OA, J_POSTM, J_IN2, J_POST2, J_PLE, J_POSTP = range(10)
    NJOB = 10
    OBLK = AW // NB
    squares = [T * (OBLK if j in (J_OA, J_OB) else NBD) for j in range(NJOB)]
    Q = [sum(squares[:j]) for j in range(NJOB + 1)]
    R_MIX, R_O, R_X2, R_PLE, R_OUT = (XU * k for k in range(5))
    CREDIT = 2
    PAIRS_B, PAIRS = BH // 2, H // 2
    NSLOT = (QB + 1) * KS
    L_KEYS = 2 * KS
    L_HEAD = L_KEYS + 2
    L_COUNT = L_KEYS + 4 * 5 + 3
    G_TAIL = (NSLOT - L_HEAD) // 2
    G_VALS = BH + AH // 2
    assert L_HEAD + 2 * (G_TAIL - 1) + 1 == NSLOT - 1 and G_TAIL - G_VALS < 4

    def slot_width(n):
        return TAIL if isinstance(n, int) and S_QKV + KS <= n < S_QKV + 2 * KS else NB

    def rows(w):
        return w[0].rearrange("(c p) n -> p c n", p=P)

    with ExitStack() as ctx:
        where = [(nc.sbuf_base + 127) // 128 * 128]

        def sb(name, shape, dt=F32):
            size = 4 if dt != BF16 else 2
            for d in shape[1:]:
                size *= d
            t = nc.alloc_sbuf_tensor_at(name, shape, dt, offset=where[0])
            where[0] += (size + 31) // 32 * 32
            return t

        def sem(name):
            return ctx.enter_context(nc.semaphore(name))

        raw = sb("raw", [P, RING, CPS, NB])
        w_high = sb("w_high", [P, RING, CPS, NB], F32R)
        w_rest = sb("w_rest", [P, RING, CPS, NB], F32R)
        x_high = sb("x_high", [P, KC, S], F32R)
        x_rest = sb("x_rest", [P, KC, S], F32R)
        resid = sb("resid", [P, T, D])
        branch = sb("branch", [P, T, D])
        silu_g = branch[:, 0, 0:T * NB].rearrange("p (t n) -> p t n", t=T)
        hidden = branch[:, 1, 0:T * NB].rearrange("p (t n) -> p t n", t=T)
        gain_row = sb("gain_row", [P, 2, NB])
        ident = sb("ident", [P, P])
        NG = 5
        G_FFN1, G_MIX, G_O, G_FFN2, G_PLE = (KC * k for k in range(NG))
        gain_T = sb("gain_T", [P, NG * KC])
        junk = sb("junk", [P, 2, NB], BF16)
        stat = sb("stat", [P, NJOB, T, NBD])
        ssum = sb("ssum", [P, NJOB, T])
        msq = sb("msq", [P, NJOB, T])
        rstd = sb("rstd", [P, NJOB, T])
        minus_half = sb("minus_half", [P, T])
        sinks = sb("sinks", [P, BH])
        spare = sb("spare", [P, 4])
        turns_from = where[0]
        h_high = sb("h_high", [P, FC, S], F32R)
        h_rest = sb("h_rest", [P, FC, S], F32R)
        turns_to = where[0]
        assert turns_to <= nc.sbuf_usable_end
        where[0] = turns_from
        z = sb("z", [P, T, ZW])
        bias_row = sb("bias_row", [P, QKV])
        vals = sb("vals", [P, T, AH + KVH, VW])
        k_swap = sb("k_swap", [P, T, KVH * HD])
        kb_T = sb("kb_T", [P, 2, S])
        qk_T = sb("qk_T", [P, 2, 2, S])
        dist_i = sb("dist_i", [P, 3 * P], I32)
        bits = sb("bits", [P, 3 * P], I32)
        dist = sb("dist", [P, 3 * P])
        count = sb("count", [P, 3 * P])
        dist_a = sb("dist_a", [P, 3 * P])
        dist_b = sb("dist_b", [P, 3 * P])
        count_T = sb("count_T", [P, 3 * P])
        score = sb("score", [P, 2, 3 * P])
        prob = sb("prob", [P, 2, 3 * P])
        PTR = 4
        prob_T = sb("prob_T", [P, PTR, 3 * P])
        peak = sb("peak", [P, 2, T])
        neg_peak = sb("neg_peak", [P, 2, T])
        neg_sinks = sb("neg_sinks", [P, BH])
        sink_e = sb("sink_e", [P, BH, T])
        denom = sb("denom", [P, 2 * T])
        assert where[0] <= turns_to
        where[0] = turns_from
        p_sb = sb("p_sb", [P, T, PLE])
        assert where[0] <= turns_from + CPS * S * 4
        p_high = sb("p_high", [P, PC, S], F32R)
        p_rest = sb("p_rest", [P, PC, S], F32R)
        emb = sb("emb", [P, T, D])
        ple_row = sb("ple_row", [P, D])
        sig = sb("sig", [P, T, NB])
        gated = sb("gated", [P, T, NB])
        assert where[0] <= turns_to
        where[0] = turns_from
        gain_in = sb("gain_in", [P, P])

        bank = [ctx.enter_context(nc.psum_tensor(f"bank{i}", [P, NB], F32)) for i in range(8)]
        acc = [bank[0:2], bank[2:4]]
        turn = bank[4:8]

        w_landed = [sem(f"w_landed{k}") for k in range(RING)]
        w_high_done, w_rest_done, w_used = sem("w_high_done"), sem("w_rest_done"), sem("w_used")
        x_landed = [sem(f"x_landed{k}") for k in range(NBD)]
        gains_landed, sinks_landed, p_landed = sem("gains_landed"), sem("sinks_landed"), sem("p_landed")
        row_landed = [sem("row_landed0"), sem("row_landed1")]
        bias_landed, mix_rows_landed = sem("bias_landed"), sem("mix_rows_landed")
        ple_row_landed, out_landed = sem("ple_row_landed"), sem("out_landed")
        pool_step, dve_step = sem("pool_step"), sem("dve_step")
        ident_ready, dist_ready = sem("ident_ready"), sem("dist_ready")
        gain_turned, gain_T_ready = sem("gain_turned"), sem("gain_T_ready")
        resid_ready = sem("resid_ready")
        turned = sem("turned")
        turn_high = sem("turn_high")
        turn_rest = sem("turn_rest")
        silu_ready, hidden_ready = sem("silu_ready"), sem("hidden_ready")
        squared, summed, rstd_ready = sem("squared"), sem("summed"), sem("rstd_ready")
        biased, branch_ready = sem("biased"), sem("branch_ready")
        z_ready, ones_ready, swap_ready = sem("z_ready"), sem("ones_ready"), sem("swap_ready")
        count_ready, count_turned, count_T_ready = sem("count_ready"), sem("count_turned"), sem("count_T_ready")
        pair_turned, pair_T_ready = sem("pair_turned"), sem("pair_T_ready")
        scored, scores_read, peak_found = sem("scored"), sem("scores_read"), sem("peak_found")
        peak_ready, prob_ready, prob_turned = sem("peak_ready"), sem("prob_ready"), sem("prob_turned")
        prob_T_a, prob_T_b = sem("prob_T_a"), sem("prob_T_b")
        weighed, o_ready = sem("weighed"), sem("o_ready")
        emb_ready, sig_ready, gated_ready = sem("emb_ready"), sem("sig_ready"), sem("gated_ready")

        def wait_prob_T(eng, h):
            if h < BH:
                eng.wait_ge(prob_T_b, h + 1)
            else:
                eng.wait_ge(prob_T_a, h - BH + 1)

        pair_bank, o_bank = bank[6], bank[7]

        def score_bank(g):
            return bank[0] if g > G_TAIL and (g - G_TAIL) % 2 else bank[4]

        def prob_bank(g):
            return bank[1] if g > G_TAIL and (g - G_TAIL) % 2 else bank[5]

        def blocks_for_pair(pr):
            if pr < PAIRS_B:
                return 2 if pr < PAIRS_B // 2 else 3
            return 5 if pr < (PAIRS_B + PAIRS) // 2 else 8

        def blocks_for_values(h):
            if h < BH:
                return 2
            return 6 if h < G_VALS else 9

        block = ctx.enter_context(nc.Block())

        @block.sync
        def _(sp):
            def load(n, k, src):
                if not (isinstance(n, int) and n < RING):
                    sp.wait_ge(w_rest_done, n - (RING - 1))
                sp.dma_start(raw[:, k, :, 0:src.shape[2]], src).then_inc(w_landed[k], 16)

            def load_block(n, w, slots, col, k0=0, s0=0, width=NB):
                v = rows(w)
                for s in range(s0, slots):
                    load(n + s, (k0 + s) % RING, v[:, CPS * s:CPS * s + CPS, bass.ds(col, width)])

            def ffn(n0, wg, wu, s0=0):
                load_block(n0, wg, KS, 0, s0=s0)
                load_block(n0 + KS, wu, KS, 0)
                with sp.Fori(1, FB) as i:
                    load_block(n0 + 2 * KS * i, wg, KS, NB * i)
                    load_block(n0 + KS + 2 * KS * i, wu, KS, NB * i)

            def down(n0, w, gain, blocks):
                with sp.Fori(0, NBD // 2) as j:
                    for h in range(2):
                        sp.wait_ge(branch_ready, CREDIT - 1 + blocks + 2 * j + h)
                        sp.dma_start(gain_row[:, h, :], gain[:, bass.ds(2 * NB * j + NB * h, NB)].to_broadcast([P, NB])
                                     ).then_inc(row_landed[h], 16)
                        load_block(n0 + FS * h + 2 * FS * j, w, FS, 2 * NB * j + NB * h, k0=FS * h)

            xv = x[0].rearrange("(t p) d -> p t d", p=P)
            for nb in range(NBD):
                sp.dma_start(resid[:, :, nb * NB:(nb + 1) * NB],
                             xv[:, :, nb * NB:(nb + 1) * NB]).then_inc(x_landed[nb], 16)
                load(nb, nb, rows(w_ffn1_gate)[:, CPS * nb:CPS * nb + CPS, 0:NB])
            ffn(S_FFN1, w_ffn1_gate, w_ffn1_up, NBD)
            down(S_DOWN1, w_ffn1_down, g_ffn1_post, 0)
            for i, (col, width) in enumerate(QKV_BLOCKS):
                if i == 0:
                    load_block(S_QKV, w_qkv, RING, col)
                    sp.wait_ge(w_used, S_QKV)
                    sp.dma_start(bias_row[:], b_qkv[:, :].to_broadcast([P, QKV])).then_inc(bias_landed, 16)
                load_block(S_QKV + KS * i, w_qkv, KS, col, s0=0 if i else RING, width=width)
            for nb in range(NBD):
                for s in range(KS):
                    if nb == 0 and s == RING:
                        sp.wait_ge(z_ready, QB + 1)
                        sp.dma_start(bias_row[:, 0:D], b_o[:, :].to_broadcast([P, D])).then_inc(mix_rows_landed, 16)
                        sp.dma_start(bias_row[:, D:2 * D], g_mix_post[:, :].to_broadcast([P, D])
                                     ).then_inc(mix_rows_landed, 16)
                    c = CPS * O_UNITS[s]
                    load(S_WO + KS * nb + s, s % RING, rows(w_o)[:, c:c + CPS, nb * NB:(nb + 1) * NB])
            ffn(S_FFN2, w_ffn2_gate, w_ffn2_up)
            down(S_DOWN2, w_ffn2_down, g_ffn2_post, 2 * NBD)
            sp.wait_ge(w_used, S_PROJ - FS + 1)
            sp.dma_start(p_sb[:], p[0, 0].rearrange("(t p) e -> p t e", p=P)).then_inc(p_landed, 16)
            for nb in range(NBD):
                load(S_PROJ + nb, nb, rows(w_ple_proj)[:, :, nb * NB:(nb + 1) * NB])
            with sp.Fori(0, NBD // 2) as j:
                for h in range(2):
                    load_block(S_GATE + KS * h + 2 * KS * j, w_ple_gate, KS, 2 * NB * j + NB * h)
            ov = out[0].rearrange("(t p) d -> p t d", p=P)
            for nb in range(NBD):
                sp.wait_ge(resid_ready, R_OUT + BPB * (nb + 1))
                sp.dma_start(ov[:, :, nb * NB:(nb + 1) * NB],
                             resid[:, :, nb * NB:(nb + 1) * NB]).then_inc(out_landed, 16)
            sp.wait_ge(out_landed, 16 * NBD)

        @block.gpsimd
        def _(pool):
            steps = [0]

            def step(ins):
                steps[0] += 1
                ins.then_inc(pool_step, 1)
                pool.wait_ge(pool_step, steps[0])

            step(nc.gpsimd.memset(ident[:], 0.0))
            nc.gpsimd.affine_select(out=ident[:], in_=ident[:], compare_op=ALU.not_equal, fill=1.0,
                                    base=0, pattern=[[-1, P]], channel_multiplier=1).then_inc(ident_ready, 1)
            step(nc.gpsimd.memset(minus_half[:], -0.5))

            def factor(job):
                by = 4.0 if job in (J_POST1, J_POST2) else 1.0
                width = AW if job in (J_OA, J_OB) else D
                pool.wait_ge(summed, job + 1)
                step(nc.gpsimd.tensor_scalar(msq[:, job, :], ssum[:, job, :], by / width, by * EPS,
                                             ALU.mult, ALU.add))
                nc.gpsimd.tensor_tensor(rstd[:, job, :], msq[:, job, :], minus_half[:], ALU.pow
                                        ).then_inc(rstd_ready, 1)

            factor(J_IN1)
            factor(J_POST1)
            factor(J_MIX)
            pool.wait_ge(w_used, S_QKV)
            nc.gpsimd.iota(dist_i[:, 0:2 * P], [[-1, 2 * P]], base=P, channel_multiplier=1).then_inc(dist_ready, 1)
            nc.gpsimd.iota(dist_i[:, 2 * P:3 * P], [[-1, P]], base=0, channel_multiplier=1).then_inc(dist_ready, 1)
            nc.gpsimd.memset(vals[:, :, :, HD:VW], 1.0).then_inc(ones_ready, 1)
            pool.wait_ge(z_ready, 2)
            for t in range(T):
                nc.gpsimd.tensor_copy(k_swap[:, t, 0:HD], z[:, t, ZKB + HD:ZKB + 2 * HD]).then_inc(swap_ready, 1)
                nc.gpsimd.tensor_copy(k_swap[:, t, HD:2 * HD], z[:, t, ZKB:ZKB + HD]).then_inc(swap_ready, 1)
            for job in (J_OB, J_OA, J_POSTM, J_IN2, J_POST2, J_PLE, J_POSTP):
                factor(job)

        @block.tensor
        def _(pe):
            def use_slot(n, k, high, rest, chunk, pair, first, last, width=NB):
                pe.wait_ge(w_rest_done, n + 1)
                for c in range(CPS):
                    for t in range(T):
                        o = pair[t][:, 0:width]
                        xh = high[:, chunk + c, t * P:(t + 1) * P]
                        xr = rest[:, chunk + c, t * P:(t + 1) * P]
                        nc.tensor.matmul(o, xh, w_high[:, k, c, 0:width], start=first and c == 0, stop=False)
                        nc.tensor.matmul(o, xh, w_rest[:, k, c, 0:width], start=False, stop=False)
                        ins = nc.tensor.matmul(o, xr, w_high[:, k, c, 0:width], start=False,
                                               stop=last and c == CPS - 1)
                ins.then_inc(w_used, 1)

            def turn_chunks(src, b):
                for c in range(CPS):
                    for t in range(T):
                        ins = nc.tensor.transpose(b[:, (c * T + t) * P:(c * T + t + 1) * P], src(t, c), ident[:])
                ins.then_inc(turned, 1)

            def turn_unit(src, u0, k, unit, sem_, need):
                pe.wait_ge(sem_, need)
                free = u0 + max(0, k - len(turn) + 1)
                if free:
                    pe.wait_ge(turn_rest, free)
                turn_chunks(lambda t, c: src(t, CPS * unit + c), turn[k % len(turn)])

            def lead_block(n0, b, u0, turn_k, units=X_UNITS, turned_before=0, width=NB):
                for k in range(turned_before, 2):
                    turn_k(k)
                for s in range(KS):
                    pe.wait_ge(turn_rest, u0 + s + 1)
                    use_slot(n0 + s, s % RING, x_high, x_rest, CPS * units[s], acc[b % 2], s == 0, s == KS - 1, width)
                    if s + 2 < KS and s + 2 >= turned_before:
                        turn_k(s + 2)

            def x_block(n0, b, units=X_UNITS, width=NB):
                for s in range(KS):
                    use_slot(n0 + s, s % RING, x_high, x_rest, CPS * units[s], acc[b % 2], s == 0, s == KS - 1, width)

            def resid_chunk(t, c):
                return resid[:, t, c * P:(c + 1) * P]

            def o_chunk(t, c):
                at = c * P if c < AW // P else ZQ + c * P - AW
                return z[:, t, at:at + P]

            def ffn(n0, b0, u_x, u_h, f):
                even, odd = acc[b0 % 2], acc[(b0 + 1) % 2]

                def turn_hidden(i):
                    pe.wait_ge(hidden_ready, f * FB + i)
                    pe.wait_ge(turn_rest, u_h - BPB + BPB * i)
                    for j in range(BPB):
                        turn_chunks(lambda t, c: hidden[:, t, (CPS * j + c) * P:(CPS * j + c + 1) * P], turn[j])

                if f:
                    pe.wait_ge(biased, T * (NBD - 1))
                    lead_block(n0, b0, u_x, lambda k: turn_unit(resid_chunk, u_x, k, k, resid_ready, R_X2 + k + 1))
                    pe.wait_ge(biased, T * NBD)
                else:
                    pe.wait_ge(gain_T_ready, 1)
                    lead_block(n0, b0, u_x, lambda k: turn_unit(resid_chunk, u_x, k, k, x_landed[k // BPB], 16))
                x_block(n0 + KS, b0 + 1)
                with pe.Fori(1, FB) as i:
                    n = n0 + 2 * KS * i
                    pe.wait_ge(silu_ready, f * FB + i)
                    for s in range(KS):
                        use_slot(n + s, s % RING, x_high, x_rest, CPS * s, even, s == 0, s == KS - 1)
                        if s == 1:
                            turn_hidden(i)
                    pe.wait_ge(hidden_ready, f * FB + i)
                    for s in range(KS):
                        use_slot(n + KS + s, s % RING, x_high, x_rest, CPS * s, odd, s == 0, s == KS - 1)
                turn_hidden(FB)

            def down(n0, b0, u_h, f):
                pe.wait_ge(silu_ready, f * FB + FB)
                with pe.Fori(0, NBD // 2) as j:
                    for h in range(2):
                        pe.wait_ge(branch_ready, CREDIT - 1 + 2 * NBD * f + 2 * j + h)
                        for s in range(FS):
                            pe.wait_ge(turn_rest, u_h + s + 1)
                            use_slot(n0 + FS * h + s + 2 * FS * j, (FS * h + s) % RING, h_high, h_rest, CPS * s,
                                     acc[(b0 + h) % 2], s == 0, s == FS - 1)

            pe.wait_ge(gains_landed, 16 * (NG + 1))
            pe.wait_ge(ident_ready, 1)
            nc.tensor.transpose(bank[0][:, 0:NG * KC], gain_in[0:NG * KC, :], ident[0:NG * KC, 0:NG * KC]
                                ).then_inc(gain_turned, 1)
            ffn(S_FFN1, 0, U_X1, U_H1, 0)
            down(S_DOWN1, 2 * FB, U_H1, 0)

            def turn_shared_keys():
                pe.wait_ge(z_ready, 2)
                pe.wait_ge(swap_ready, 2 * T)
                pe.wait_ge(turn_rest, U_MIX + XU)
                for t in range(T):
                    nc.tensor.transpose(pair_bank[:, t * P:(t + 1) * P], z[:, t, ZKB:ZKB + P], ident[:])
                for t in range(T):
                    ins = nc.tensor.transpose(pair_bank[:, S + t * P:S + (t + 1) * P], k_swap[:, t, :], ident[:])
                ins.then_inc(pair_turned, 1)

            def turn_pair(pr):
                pe.wait_ge(z_ready, blocks_for_pair(pr))
                pe.wait_ge(pair_T_ready, pr + 1)
                if pr == 6:
                    pe.wait_ge(count_T_ready, 1)
                at = ZQ + pr * P if pr < PAIRS_B else (pr - PAIRS_B) * P
                for t in range(T):
                    ins = nc.tensor.transpose(pair_bank[:, t * P:(t + 1) * P], z[:, t, at:at + P], ident[:])
                if pr >= PAIRS_B:
                    for t in range(T):
                        ins = nc.tensor.transpose(pair_bank[:, S + t * P:S + (t + 1) * P],
                                                  z[:, t, ZK + at:ZK + at + P], ident[:])
                ins.then_inc(pair_turned, 1)

            def turn_count():
                pe.wait_ge(count_ready, 1)
                pe.wait_ge(pair_T_ready, 7)
                for c in range(3):
                    ins = nc.tensor.transpose(pair_bank[:, c * P:(c + 1) * P], count[:, c * P:(c + 1) * P], ident[:])
                ins.then_inc(count_turned, 1)

            def scores(g):
                pe.wait_ge(pair_T_ready, g // 2 + 2)
                if g > G_TAIL:
                    pe.wait_ge(scores_read, g - 1)
                    pe.wait_ge(z_ready, QB + 1)
                elif g:
                    pe.wait_ge(scores_read, g)
                lo = HD * (g % 2)
                q = qk_T[lo:lo + HD, (g // 2) % 2, 0, :]
                if g < BH:
                    k = kb_T[lo:lo + HD, (g // (BH // KVH) + g) % 2, :]
                else:
                    k = qk_T[lo:lo + HD, (g // 2) % 2, 1, :]
                b = score_bank(g)
                nc.tensor.matmul(b[:, 0:S], q[:, P:S], k, start=True, stop=True)
                nc.tensor.matmul(b[:, S:S + P], q[:, 0:P], k[:, 0:P], start=True, stop=True).then_inc(scored, 1)

            def turn_prob(h):
                pe.wait_ge(prob_ready, h + 1)
                if h > G_TAIL:
                    if h > G_TAIL + 1:
                        wait_prob_T(pe, h - 2)
                elif h:
                    wait_prob_T(pe, h - 1)
                for c in range(3):
                    ins = nc.tensor.transpose(prob_bank(h)[:, c * P:(c + 1) * P],
                                              prob[:, h % 2, c * P:(c + 1) * P], ident[:])
                ins.then_inc(prob_turned, 1)

            def weigh(h):
                wait_prob_T(pe, h)
                pe.wait_ge(z_ready, blocks_for_values(h))
                pe.wait_ge(ones_ready, 1)
                if h % 2 == 0 and h:
                    pe.wait_ge(o_ready, h // 2)
                v = AH + h // (BH // KVH) if h < BH else h - BH
                w = prob_T[:, h % PTR, :]
                o = [o_bank[:, (h % 2 * T + t) * VW:(h % 2 * T + t + 1) * VW] for t in range(T)]
                nc.tensor.matmul(o[1], w[:, 0:P], vals[:, 0, v, :], start=True, stop=False)
                nc.tensor.matmul(o[1], w[:, P:2 * P], vals[:, 1, v, :], start=False, stop=True)
                nc.tensor.matmul(o[0], w[:, 2 * P:3 * P], vals[:, 0, v, :], start=True, stop=True
                                 ).then_inc(weighed, 1)

            def turn_mix(k):
                turn_unit(resid_chunk, U_MIX, k, k, resid_ready, R_MIX + k + 1)

            turn_mix(0)
            turn_mix(1)
            for L in range(NSLOT):
                i, s = divmod(L, KS)
                if i == 0:
                    pe.wait_ge(turn_rest, U_MIX + s + 1)
                if i >= 2 and s == 0:
                    pe.wait_ge(z_ready, i - 1)
                use_slot(S_QKV + L, s % RING, x_high, x_rest, CPS * s, acc[(B_QKV + i) % 2], s == 0, s == KS - 1,
                         QKV_BLOCKS[i][1])
                if L + 2 < XU:
                    turn_mix(L + 2)
                g = (L - L_HEAD) // 2
                if L == L_KEYS:
                    turn_shared_keys()
                elif L >= L_HEAD and L % 2 == 0:
                    if 0 < g <= G_VALS:
                        weigh(g - 1)
                    scores(g)
                elif L > L_KEYS:
                    if g >= 0:
                        turn_prob(g)
                    if (L - L_KEYS) % 4 == 1:
                        turn_pair((L - L_KEYS) // 4)
                    if L == L_COUNT:
                        turn_count()
            for g in range(G_TAIL, H + 3):
                if g < H:
                    if g // 2 * 2 + 1 == g and g // 2 + 1 < PAIRS:
                        turn_pair(g // 2 + 1)
                    scores(g)
                if G_TAIL < g <= H:
                    turn_prob(g - 1)
                weigh(g - 3)
            def turn_o(k):
                turn_unit(o_chunk, U_O, k, O_UNITS[k], resid_ready, R_O + k + 1)

            pe.wait_ge(o_ready, PAIRS)
            lead_block(S_WO, B_WO, U_O, turn_o, O_UNITS)
            for nb in range(1, NBD):
                if nb >= 2:
                    pe.wait_ge(biased, T * (nb - 1))
                x_block(S_WO + KS * nb, B_WO + nb, O_UNITS)
            ffn(S_FFN2, B_FFN2, U_X2, U_H2, 1)
            down(S_DOWN2, B_FFN2 + 2 * FB, U_H2, 1)
            def turn_ple(k):
                turn_unit(resid_chunk, U_PLE, k, k, resid_ready, R_PLE + k + 1)

            pe.wait_ge(p_landed, 16)
            pe.wait_ge(turn_rest, U_P)
            turn_chunks(lambda t, c: p_sb[:, t, c * P:(c + 1) * P], turn[len(turn) - 1])
            pe.wait_ge(turn_rest, U_PLE)
            for nb in range(NBD):
                if nb < 2:
                    pe.wait_ge(branch_ready, CREDIT + 3 * NBD - 1 + nb)
                else:
                    pe.wait_ge(emb_ready, nb - 1)
                use_slot(S_PROJ + nb, nb, p_high, p_rest, 0, acc[(B_PROJ + nb) % 2], True, True)
                if nb >= 2:
                    turn_ple(nb - 2)
            pe.wait_ge(emb_ready, NBD - 1)
            lead_block(S_GATE, B_GATE, U_PLE, turn_ple, turned_before=2)
            for nb in range(1, NBD):
                if nb == 1:
                    pe.wait_ge(emb_ready, NBD)
                else:
                    pe.wait_ge(sig_ready, T * (nb - 1))
                x_block(S_GATE + KS * nb, B_GATE + nb)

        @block.scalar
        def _(act):
            def high(n, k):
                if isinstance(n, int) and n >= S_END:
                    return
                act.wait_ge(w_landed[k], 4 * n - 4 * k + 16)
                if not (isinstance(n, int) and n < RING):
                    act.wait_ge(w_used, n - (RING - 1))
                width = slot_width(n)
                nc.scalar.copy(w_high[:, k, :, 0:width], raw[:, k, :, 0:width]).then_inc(w_high_done, 1)

            def ahead(n, s0, count_, k0=0):
                for s in range(s0, s0 + count_):
                    high(n + s + RING, (k0 + s) % RING)

            def square(q, src, job, t, b):
                if not (isinstance(q, int) and q < 2):
                    act.wait_ge(squared, q - 1)
                nc.scalar.activation(junk[:, t % 2, :], src, ACT.Square, accum_out=stat[:, job, t, b]
                                     ).then_inc(squared, 1)

            def col(b):
                return slice(b, b + 1)

            def blk(b):
                return slice(b * NB, (b + 1) * NB)

            def x_unit(u0, k, unit, gain):
                act.wait_ge(turned, u0 + k + 1)
                for c in range(CPS):
                    ch = CPS * unit + c
                    ins = nc.scalar.activation(x_high[:, ch, :], turn[k % len(turn)][:, c * S:(c + 1) * S],
                                               ACT.Copy, scale=gain_T[:, gain + ch:gain + ch + 1])
                ins.then_inc(turn_high, 1)

            def square_resid(job, nb):
                for t in range(T):
                    square(Q[job] + T * nb + t, resid[:, t, blk(nb)], job, t, col(nb))

            def boundary(u0, gain, n0, job):
                for k in range(XU):
                    x_unit(u0, k, k, gain)
                    if k >= RING:
                        high(n0 + k, k % RING)
                    if k % BPB == 1:
                        square_resid(job, k // BPB)

            def ffn(n0, b0, u_h, job):
                def silu(i):
                    act.wait_ge(w_used, n0 + KS + 2 * KS * i)
                    for t in range(T):
                        ins = nc.scalar.activation(silu_g[:, t, :], acc[b0 % 2][t][:], ACT.Silu,
                                                   scale=rstd[:, job, t:t + 1])
                    ins.then_inc(silu_ready, 1)

                def hidden_high(i):
                    for j in range(BPB):
                        act.wait_ge(turned, u_h - BPB + j + 1 + BPB * i)
                        nc.scalar.copy(h_high[:, bass.ds(CB * i - CB + CPS * j, CPS), :],
                                       turn[j][:].rearrange("p (c s) -> p c s", c=CPS)).then_inc(turn_high, 1)

                ahead(n0, KS - RING, RING - 1)
                act.wait_ge(rstd_ready, job + 1)
                silu(0)
                ahead(n0, KS - 1, KS + 1)
                with act.Fori(1, FB) as i:
                    n = n0 + 2 * KS * i
                    ahead(n, 0, 3)
                    hidden_high(i)
                    ahead(n, 3, KS - 4)
                    silu(i)
                    ahead(n, KS - 1, KS + 1)
                hidden_high(FB)

            def down(n0, b0, job):
                for nb in range(NBD):
                    n = n0 + FS * nb
                    ahead(n, 0, FS - 1, FS * nb)
                    act.wait_ge(w_used, n + FS)
                    for t in range(T):
                        square(Q[job] + T * nb + t, acc[(b0 + nb) % 2][t][:], job, t, col(nb))
                    ahead(n, FS - 1, 1, FS * nb)

            for n, g in enumerate((g_ffn1_pre, g_mix_pre, None, g_ffn2_pre, g_ple_pre)):
                for src, at in [(g_out_a, 0), (g_out_b, AW // P)] if g is None else [(g, 0)]:
                    v = src[0].rearrange("(c p) -> c p", p=P)
                    act.dma_start(gain_in[n * KC + at:n * KC + at + v.shape[0], :], v).then_inc(gains_landed, 16)
            act.dma_start(sinks[:], attn_sinks.rearrange("a k g -> a (k g)").to_broadcast([P, BH])
                          ).then_inc(sinks_landed, 16)
            act.wait_ge(gain_T_ready, 1)
            for k in range(XU):
                x_unit(U_X1, k, k, G_FFN1)
                high(k, k % RING)
                if k % BPB == 1:
                    square_resid(J_IN1, k // BPB)
            ffn(S_FFN1, 0, U_H1, J_IN1)
            down(S_DOWN1, 2 * FB, J_POST1)
            boundary(U_MIX, G_MIX, S_QKV, J_MIX)

            def pair_out(pr):
                act.wait_ge(pair_turned, pr + 2)
                if pr >= 2:
                    act.wait_ge(scored, 2 * pr - 2)
                n = 1 if pr < PAIRS_B else 2
                nc.scalar.copy(qk_T[:, pr % 2, 0:n, :], pair_bank[:, 0:n * S].rearrange("p (n s) -> p n s", n=n)
                               ).then_inc(pair_T_ready, 1)

            def exps(g):
                act.wait_ge(peak_ready, g + 1)
                if g >= 2:
                    act.wait_ge(prob_turned, g - 1)
                nc.scalar.activation(prob[:, g % 2, 0:S], score[:, g % 2, 0:S], ACT.Exp,
                                     bias=neg_peak[:, g % 2, 1:2], scale=HD ** -0.5)
                if g < BH:
                    nc.scalar.activation(sink_e[:, g, :], neg_peak[:, g % 2, :], ACT.Exp, bias=sinks[:, g:g + 1])
                nc.scalar.activation(prob[:, g % 2, S:S + P], score[:, g % 2, S:S + P], ACT.Exp,
                                     bias=neg_peak[:, g % 2, 0:1], scale=HD ** -0.5).then_inc(prob_ready, 1)

            def prob_T_out(h):
                act.wait_ge(prob_turned, h + 1)
                if h >= PTR:
                    act.wait_ge(weighed, h - PTR + 1)
                nc.scalar.copy(prob_T[:, h % PTR, :], prob_bank(h)[:, 0:3 * P]).then_inc(prob_T_b, 1)

            def square_o(job, b, t):
                at = (ZQ if job == J_OB else 0) + b * NB
                square(Q[job] + T * b + t, z[:, t, at:at + NB], job, t, col(b))

            act.wait_ge(sinks_landed, 16)
            for L in range(NSLOT):
                if L >= KS - RING:
                    high(S_QKV + L + RING, L % RING)
                g = (L - L_HEAD) // 2
                if L == L_KEYS:
                    act.wait_ge(pair_turned, 1)
                    nc.scalar.copy(kb_T[:].rearrange("p a s -> p (a s)"), pair_bank[:]).then_inc(pair_T_ready, 1)
                elif L >= L_HEAD and L % 2 == 0:
                    exps(g)
                elif L > L_KEYS:
                    if 0 <= g < BH:
                        prob_T_out(g)
                    if (L - L_KEYS) % 4 == 1:
                        pair_out((L - L_KEYS) // 4)
                for m in range(T * OBLK):
                    if L == L_HEAD + 2 * BH + 3 + 2 * m:
                        act.wait_ge(o_ready, BH // 2)
                        square_o(J_OB, m // T, m % T)
            for g in range(G_TAIL, H):
                if g // 2 * 2 + 1 == g and g // 2 + 1 < PAIRS:
                    pair_out(g // 2 + 1)
                exps(g)
                if g == G_TAIL + 1:
                    act.wait_ge(o_ready, G_VALS // 2)
                    for t in range(T):
                        square_o(J_OA, 0, t)
            act.wait_ge(o_ready, PAIRS)
            for t in range(T):
                square_o(J_OA, 1, t)
            for k in range(XU):
                x_unit(U_O, k, O_UNITS[k], G_O)
                if k >= RING:
                    high(S_WO + k, k % RING)
            for nb in range(NBD):
                n = S_WO + KS * nb
                ahead(n, 0 if nb else KS - RING, KS - 1 if nb else RING - 1)
                for t in range(T):
                    act.wait_ge(biased, T * nb + t + 1)
                    square(Q[J_POSTM] + T * nb + t, branch[:, t, blk(nb)], J_POSTM, t, col(nb))
                ahead(n, KS - 1, 1)
            boundary(U_X2, G_FFN2, S_FFN2, J_IN2)
            ffn(S_FFN2, B_FFN2, U_H2, J_IN2)
            down(S_DOWN2, B_FFN2 + 2 * FB, J_POST2)
            act.wait_ge(turned, U_P + 1)
            nc.scalar.copy(p_high[:].rearrange("p c s -> p (c s)"), turn[len(turn) - 1][:]).then_inc(turn_high, 1)
            act.dma_start(ple_row[:], g_ple_post[:, :].to_broadcast([P, D])).then_inc(ple_row_landed, 16)
            for nb in range(NBD):
                act.wait_ge(w_used, S_PROJ + nb + 1)
                for t in range(T):
                    ins = nc.scalar.copy(emb[:, t, blk(nb)], acc[(B_PROJ + nb) % 2][t][:])
                ins.then_inc(emb_ready, 1)
                high(S_GATE + nb, nb)
                if nb >= 2:
                    x_unit(U_PLE, nb - 2, nb - 2, G_PLE)
            for k in range(2, XU):
                x_unit(U_PLE, k, k, G_PLE)
                if k >= RING:
                    high(S_GATE + k, k % RING)
            for nb in range(NBD):
                square_resid(J_PLE, nb)
            for nb in range(NBD):
                n = S_GATE + KS * nb
                ahead(n, 0 if nb else KS - RING, KS - 1 if nb else RING - 1)
                act.wait_ge(rstd_ready, J_PLE + 1)
                act.wait_ge(w_used, n + KS)
                if nb:
                    act.wait_ge(gated_ready, T * nb)
                for t in range(T):
                    ins = nc.scalar.activation(sig[:, t, :], acc[(B_GATE + nb) % 2][t][:], ACT.Sigmoid,
                                               scale=rstd[:, J_PLE, t:t + 1])
                    ins.then_inc(sig_ready, 1)
                ahead(n, KS - 1, 1)
                for t in range(T):
                    act.wait_ge(gated_ready, T * nb + t + 1)
                    square(Q[J_POSTP] + T * nb + t, gated[:, t, :], J_POSTP, t, col(nb))

        @block.vector
        def _(dve):
            steps = [0]

            def step(ins):
                steps[0] += 1
                ins.then_inc(dve_step, 1)
                dve.wait_ge(dve_step, steps[0])

            def rest(n, k):
                if isinstance(n, int) and n >= S_END:
                    return
                dve.wait_ge(w_high_done, n + 1)
                width = slot_width(n)
                nc.vector.tensor_tensor(w_rest[:, k, :, 0:width], raw[:, k, :, 0:width],
                                        w_high[:, k, :, 0:width].bitcast(F32), ALU.subtract).then_inc(w_rest_done, 1)

            def ahead(n, s0, count_, k0=0):
                for s in range(s0, s0 + count_):
                    rest(n + s + RING, (k0 + s) % RING)

            def blk(b):
                return slice(b * NB, (b + 1) * NB)

            def reduce(job):
                dve.wait_ge(squared, Q[job + 1])
                nc.vector.reduce_sum(ssum[:, job, :], stat[:, job, :, 0:squares[job] // T], axis=AX.X
                                     ).then_inc(summed, 1)

            def x_rest_unit(u0, k, unit, gain):
                dve.wait_ge(turn_high, u0 + k + 1)
                for c in range(CPS):
                    ch = CPS * unit + c
                    ins = nc.vector.scalar_tensor_tensor(
                        out=x_rest[:, ch, :], in0=turn[k % len(turn)][:, c * S:(c + 1) * S],
                        scalar=gain_T[:, gain + ch:gain + ch + 1], in1=x_high[:, ch, :].bitcast(F32),
                        op0=ALU.mult, op1=ALU.subtract)
                ins.then_inc(turn_rest, 1)

            def add_branch(job):
                def update(k):
                    at = slice(k * UW, (k + 1) * UW)
                    for t in range(T):
                        ins = nc.vector.scalar_tensor_tensor(out=resid[:, t, at], in0=branch[:, t, at],
                                                             scalar=rstd[:, job, t:t + 1], in1=resid[:, t, at],
                                                             op0=ALU.mult, op1=ALU.add)
                    ins.then_inc(resid_ready, 1)
                return update

            def boundary(u0, gain, n0, update):
                update(0)
                for k in range(XU):
                    if k + 1 < XU:
                        update(k + 1)
                    x_rest_unit(u0, k, k, gain)
                    if k >= RING:
                        rest(n0 + k, k % RING)

            def ffn(n0, b0, u_h, job, f):
                def gate_up(i):
                    dve.wait_ge(w_used, n0 + 2 * KS + 2 * KS * i)
                    dve.wait_ge(silu_ready, f * FB + 1 + i)
                    for t in range(T):
                        ins = nc.vector.scalar_tensor_tensor(out=hidden[:, t, :], in0=acc[(b0 + 1) % 2][t][:],
                                                             scalar=rstd[:, job, t:t + 1], in1=silu_g[:, t, :],
                                                             op0=ALU.mult, op1=ALU.mult)
                    ins.then_inc(hidden_ready, 1)

                def hidden_rest(i):
                    for j in range(BPB):
                        chunks = bass.ds(CB * i - CB + CPS * j, CPS)
                        dve.wait_ge(turn_high, u_h - BPB + j + 1 + BPB * i)
                        nc.vector.tensor_tensor(h_rest[:, chunks, :], turn[j][:].rearrange("p (c s) -> p c s", c=CPS),
                                                h_high[:, chunks, :].bitcast(F32), ALU.subtract).then_inc(turn_rest, 1)

                ahead(n0, KS - RING, KS + RING - 1)
                dve.wait_ge(rstd_ready, job + 1)
                gate_up(0)
                ahead(n0, 2 * KS - 1, 1)
                with dve.Fori(1, FB) as i:
                    n = n0 + 2 * KS * i
                    ahead(n, 0, 3)
                    hidden_rest(i)
                    ahead(n, 3, 2 * KS - 4)
                    gate_up(i)
                    ahead(n, 2 * KS - 1, 1)
                hidden_rest(FB)

            def down(n0, b0, job, f):
                for nb in range(NBD):
                    n = n0 + FS * nb
                    ahead(n, 0, FS - 1, FS * nb)
                    dve.wait_ge(row_landed[nb % 2], 16 * (2 * f + nb // 2 + 1))
                    for t in range(T):
                        if nb == NBD - 1 and t == T - 1:
                            reduce(job)
                        dve.wait_ge(squared, Q[job] + T * nb + t + 1)
                        ins = nc.vector.tensor_tensor(branch[:, t, blk(nb)], acc[(b0 + nb) % 2][t][:],
                                                      gain_row[:, nb % 2, :], ALU.mult)
                    ins.then_inc(branch_ready, 1)
                    ahead(n, FS - 1, 1, FS * nb)
                dve.wait_ge(branch_ready, CREDIT + (2 * f + 1) * NBD)
                dve.wait_ge(rstd_ready, job + 1)

            nc.vector.memset(spare[:, 0:1], 0.0).then_inc(branch_ready, CREDIT)
            dve.wait_ge(gain_turned, 1)
            nc.vector.tensor_copy(gain_T[:], bank[0][:, 0:NG * KC]).then_inc(gain_T_ready, 1)
            dve.wait_ge(gain_T_ready, 1)
            for k in range(XU):
                x_rest_unit(U_X1, k, k, G_FFN1)
                rest(k, k % RING)
            reduce(J_IN1)
            ffn(S_FFN1, 0, U_H1, J_IN1, 0)
            down(S_DOWN1, 2 * FB, J_POST1, 0)
            boundary(U_MIX, G_MIX, S_QKV, add_branch(J_POST1))
            reduce(J_MIX)

            def project_out(i):
                col, width = QKV_BLOCKS[i]
                dve.wait_ge(w_used, S_QKV + KS * (i + 1))
                if col < 2 * AW:
                    parts = [(0, width, col, None)]
                elif col < QH:
                    parts = [(0, width, None, (col - 2 * AW) // HD)]
                elif col < KB:
                    parts = [(0, width, ZQ + col - QH, None)]
                else:
                    parts = [(0, VB - KB, ZKB, None), (VB - KB, width, None, AH)]
                for at, to, dst, head in parts:
                    for t in range(T):
                        src, b = acc[(B_QKV + i) % 2][t][:, at:to], bias_row[:, col + at:col + to]
                        if head is None:
                            o = z[:, t, dst:dst + to - at]
                        else:
                            o = vals[:, t, head:head + (to - at) // HD, 0:HD]
                            src = src.rearrange("p (h d) -> p h d", d=HD)
                            b = b.rearrange("p (h d) -> p h d", d=HD)
                        ins = nc.vector.scalar_tensor_tensor(out=o, in0=src, scalar=rstd[:, J_MIX, t:t + 1], in1=b,
                                                             op0=ALU.mult, op1=ALU.add)
                ins.then_inc(z_ready, 1)

            def table_b():
                dve.wait_ge(dist_ready, 2)
                step(nc.vector.tensor_copy(dist[:], dist_i[:]))
                step(nc.vector.tensor_scalar(dist_b[:], dist[:], 0.0, BIG, ALU.is_lt, ALU.mult))
                step(nc.vector.tensor_scalar(count[:], dist[:], float(P), BIG, ALU.is_ge, ALU.mult))
                step(nc.vector.tensor_tensor(dist_b[:], dist_b[:], count[:], ALU.add))
                step(nc.vector.tensor_tensor(dist_b[:], dist_b[:], dist[:], ALU.add))
                dve.wait_ge(sinks_landed, 16)
                step(nc.vector.tensor_scalar(neg_sinks[:], sinks[:], -1.0, None, ALU.mult))

            def table_near():
                step(nc.vector.tensor_scalar(count[:], dist[:], float(P), None, ALU.is_le))

            def table_dilated(dil):
                step(nc.vector.tensor_scalar(bits[:], dist_i[:], dil - 1, None, ALU.bitwise_and))
                step(nc.vector.tensor_copy(dist_a[:], bits[:]))
                step(nc.vector.scalar_tensor_tensor(out=count[:], in0=dist_a[:], scalar=0.0, in1=count[:],
                                                    op0=ALU.is_equal, op1=ALU.add))

            def table_count():
                nc.vector.scalar_tensor_tensor(out=count[:], in0=dist[:], scalar=0.0, in1=count[:],
                                               op0=ALU.is_ge, op1=ALU.mult).then_inc(count_ready, 1)
                dve.wait_ge(count_ready, 1)

            def table_a():
                step(nc.vector.tensor_scalar(dist_a[:], count[:], 0.0, BIG, ALU.is_equal, ALU.mult))
                step(nc.vector.tensor_tensor(dist_a[:], dist_a[:], dist[:], ALU.add))

            def soften(g):
                dve.wait_ge(scored, g + 1)
                if g >= 2:
                    dve.wait_ge(prob_ready, g - 1)
                nc.vector.scalar_tensor_tensor(out=score[:, g % 2, :], in0=(dist_b if g < BH else dist_a)[:],
                                               scalar=-head_slope[g] * HD ** 0.5, in1=score_bank(g)[:, 0:3 * P],
                                               op0=ALU.mult, op1=ALU.add).then_inc(scores_read, 1)
                dve.wait_ge(scores_read, g + 1)
                nc.vector.reduce_max(peak[:, g % 2, 1:2], score[:, g % 2, 0:S], axis=AX.X)
                nc.vector.reduce_max(peak[:, g % 2, 0:1], score[:, g % 2, S:S + P], axis=AX.X
                                     ).then_inc(peak_found, 1)
                dve.wait_ge(peak_found, g + 1)
                if g < BH:
                    ins = nc.vector.tensor_scalar(neg_peak[:, g % 2, :], peak[:, g % 2, :], -HD ** -0.5,
                                                  neg_sinks[:, g:g + 1], ALU.mult, ALU.min)
                else:
                    ins = nc.vector.tensor_scalar(neg_peak[:, g % 2, :], peak[:, g % 2, :], -HD ** -0.5, None, ALU.mult)
                ins.then_inc(peak_ready, 1)

            def prob_T_out(h):
                dve.wait_ge(prob_turned, h + 1)
                dve.wait_ge(weighed, h - PTR + 1)
                nc.vector.tensor_tensor(prob_T[:, h % PTR, :], prob_bank(h)[:, 0:3 * P], count_T[:], ALU.mult
                                        ).then_inc(prob_T_a, 1)

            def pair_o(q):
                dve.wait_ge(weighed, 2 * (q + 1))
                o = o_bank[:, 0:2 * T * VW].rearrange("p (n c) -> p n c", c=VW)
                if q < PAIRS_B:
                    step(nc.vector.tensor_tensor(denom[:], o[:, :, HD],
                                                 sink_e[:, 2 * q:2 * q + 2, :].rearrange("p h t -> p (h t)"), ALU.add))
                    step(nc.vector.reciprocal(denom[:], denom[:]))
                    at = ZQ + q * P
                else:
                    step(nc.vector.reciprocal(denom[:], o[:, :, HD]))
                    at = (q - PAIRS_B) * P
                o4 = o_bank[:, 0:2 * T * VW].rearrange("p (h t c) -> p h t c", h=2, t=T)
                nc.vector.tensor_tensor(
                    z[:, :, at:at + P].rearrange("p t (h d) -> p h t d", h=2), o4[:, :, :, 0:HD],
                    denom[:].rearrange("p (h t) -> p h t", h=2).unsqueeze(3).to_broadcast([P, 2, T, HD]), ALU.mult
                    ).then_inc(o_ready, 1)

            def scale_o(k):
                unit = O_UNITS[k]
                job = J_OA if unit < XU // 2 else J_OB
                at = unit * UW if unit < XU // 2 else ZQ - AW + unit * UW
                for t in range(T):
                    ins = nc.vector.tensor_scalar(z[:, t, at:at + UW], z[:, t, at:at + UW], rstd[:, job, t:t + 1],
                                                  None, ALU.mult)
                ins.then_inc(resid_ready, 1)

            for L in range(NSLOT):
                i, s = divmod(L, KS)
                g = (L - L_HEAD) // 2
                if L >= L_HEAD:
                    if L % 2 == 0:
                        soften(g)
                    else:
                        if g >= 2 and g % 2 == 0 and g <= G_VALS:
                            pair_o(g // 2 - 1)
                        if g >= BH:
                            prob_T_out(g)
                if L == KS:
                    table_b()
                if L == L_HEAD + 1:
                    table_near()
                if L == L_HEAD + 5:
                    table_dilated(4)
                if L == L_HEAD + 9:
                    table_dilated(16)
                if L == L_HEAD + 13:
                    table_count()
                if L == L_HEAD + 17:
                    table_a()
                if L == L_COUNT:
                    dve.wait_ge(count_turned, 1)
                    step(nc.vector.tensor_copy(count_T[:], pair_bank[:, 0:3 * P]))
                    nc.vector.memset(spare[:, 1:2], 0.0).then_inc(count_T_ready, 1)
                if L == L_HEAD + 2 * BH + 4 + 2 * T * OBLK:
                    reduce(J_OB)
                if L == L_HEAD + 2 * BH + 6 + 2 * T * OBLK:
                    dve.wait_ge(rstd_ready, J_OB + 1)
                    dve.wait_ge(o_ready, PAIRS_B)
                    for k in range(XU // 2):
                        scale_o(k)
                if s == KS - 1:
                    if i == 0:
                        dve.wait_ge(rstd_ready, J_MIX + 1)
                        dve.wait_ge(bias_landed, 16)
                    project_out(i)
                if L >= KS - RING:
                    rest(S_QKV + L + RING, s % RING)
            for g in range(G_TAIL, H + 3):
                if g < H:
                    soften(g)
                if G_TAIL < g <= H:
                    prob_T_out(g - 1)
                if g % 2 == 0:
                    pair_o((g - 4) // 2)
            reduce(J_OA)
            x_rest_unit(U_O, 0, O_UNITS[0], G_O)
            x_rest_unit(U_O, 1, O_UNITS[1], G_O)
            dve.wait_ge(rstd_ready, J_OA + 1)
            dve.wait_ge(o_ready, PAIRS)
            for k in range(2, XU):
                if k + XU // 2 - 2 < XU:
                    scale_o(k + XU // 2 - 2)
                x_rest_unit(U_O, k, O_UNITS[k], G_O)
                if k >= RING:
                    rest(S_WO + k, k % RING)
            dve.wait_ge(mix_rows_landed, 32)

            def gain_mix(nb, last):
                for t in range(T):
                    if last and t == T - 1:
                        reduce(J_POSTM)
                    dve.wait_ge(squared, Q[J_POSTM] + T * nb + t + 1)
                    ins = nc.vector.tensor_tensor(branch[:, t, blk(nb)], branch[:, t, blk(nb)],
                                                  bias_row[:, D + nb * NB:D + (nb + 1) * NB], ALU.mult)
                ins.then_inc(branch_ready, 1)

            for nb in range(NBD):
                n = S_WO + KS * nb
                for s in range(0 if nb else KS - RING, KS):
                    if nb and s == 3:
                        gain_mix(nb - 1, False)
                    if s == KS - 1:
                        dve.wait_ge(w_used, n + KS)
                        for t in range(T):
                            nc.vector.tensor_tensor(branch[:, t, blk(nb)], acc[(B_WO + nb) % 2][t][:],
                                                    bias_row[:, blk(nb)], ALU.add).then_inc(biased, 1)
                    rest(n + s + RING, s % RING)
            gain_mix(NBD - 1, True)
            dve.wait_ge(branch_ready, CREDIT + 2 * NBD)
            dve.wait_ge(rstd_ready, J_POSTM + 1)
            boundary(U_X2, G_FFN2, S_FFN2, add_branch(J_POSTM))
            reduce(J_IN2)
            ffn(S_FFN2, B_FFN2, U_H2, J_IN2, 1)
            down(S_DOWN2, B_FFN2 + 2 * FB, J_POST2, 1)
            update = add_branch(J_POST2)
            update(0)
            dve.wait_ge(turn_high, U_P + 1)
            nc.vector.tensor_tensor(p_rest[:].rearrange("p c s -> p (c s)"), turn[len(turn) - 1][:],
                                    p_high[:].rearrange("p c s -> p (c s)").bitcast(F32), ALU.subtract
                                    ).then_inc(turn_rest, 1)
            for k in range(XU):
                if k + 1 < XU:
                    update(k + 1)
                if k < RING:
                    rest(S_GATE + k, k)
                x_rest_unit(U_PLE, k, k, G_PLE)
                if k >= RING:
                    rest(S_GATE + k, k % RING)
            reduce(J_PLE)
            dve.wait_ge(ple_row_landed, 16)
            for nb in range(NBD):
                n = S_GATE + KS * nb
                ahead(n, 0 if nb else KS - RING, KS - 1 if nb else RING - 1)
                for t in range(T):
                    dve.wait_ge(sig_ready, T * nb + t + 1)
                    if nb:
                        dve.wait_ge(squared, Q[J_POSTP] + T * (nb - 1) + t + 1)
                    nc.vector.tensor_tensor(gated[:, t, :], sig[:, t, :], emb[:, t, blk(nb)], ALU.mult
                                            ).then_inc(gated_ready, 1)
                for t in range(T):
                    dve.wait_ge(gated_ready, T * nb + t + 1)
                    ins = nc.vector.tensor_tensor(branch[:, t, blk(nb)], gated[:, t, :], ple_row[:, blk(nb)], ALU.mult)
                ins.then_inc(branch_ready, 1)
                ahead(n, KS - 1, 1)
            reduce(J_POSTP)
            dve.wait_ge(branch_ready, CREDIT + 4 * NBD)
            dve.wait_ge(rstd_ready, J_POSTP + 1)
            update = add_branch(J_POSTP)
            for k in range(XU):
                update(k)


_OUT = (1, 256, 2048)


def kernel(**inputs):
    import numpy as _np
    import concourse.bacc as _bacc
    from concourse.bass_utils import run_bass_kernel_spmd as _run

    nc = _bacc.Bacc("TRN2", target_bir_lowering=False, num_devices=1)
    arrays, args = {}, {}
    for name, value in inputs.items():
        a = _np.ascontiguousarray(value)
        arrays[f"in_{name}"] = a
        args[name] = nc.dram_tensor(f"in_{name}", a.shape, mybir.dt.from_np(a.dtype), kind="ExternalInput").ap()
    out = nc.dram_tensor("out_h", _OUT, F32, kind="ExternalOutput").ap()
    layer_program(nc, out=out, **args)
    r = _run(nc, [arrays], core_ids=[0])
    return r.results[0]["out_h"]
```

```python
from contextlib import ExitStack

import concourse.bass as bass
from concourse import mybir

F32 = mybir.dt.float32
F32R = mybir.dt.float32r
BF16 = mybir.dt.bfloat16
I32 = mybir.dt.int32
ALU = mybir.AluOpType
ACT = mybir.ActivationFunctionType
AX = mybir.AxisListType

P = 128
NB = 512
RING = 4
CPS = 2
EPS = 1e-6
HD = 64
WARM_1, WARM_2, WARM_MIX, WARM_X2, WARM_3 = 6, 6, 10, 16, 5
EARLY, EARLY_MIX = 3, 1
BIG = 1e30
VW = HD + 2


def layer_program(nc, x, p, g_ffn1_pre, w_ffn1_gate, w_ffn1_up, w_ffn1_down, g_ffn1_post,
                  g_mix_pre, w_qkv, b_qkv, attn_sinks, g_out_a, g_out_b, w_o, b_o, g_mix_post,
                  g_ffn2_pre, w_ffn2_gate, w_ffn2_up, w_ffn2_down, g_ffn2_post,
                  g_ple_pre, w_ple_gate, w_ple_proj, g_ple_post, out):
    _, S, D = x.shape
    F = w_ffn1_gate.shape[2]
    QKV = w_qkv.shape[2]
    PLE = p.shape[3]
    AW = g_out_a.shape[1]
    AH = AW // HD
    BH = attn_sinks.shape[1] * attn_sinks.shape[2]
    KVH = attn_sinks.shape[1]
    H = AH + BH
    T = S // P
    KC = D // P
    FC = F // P
    NBD = D // NB
    FB = F // NB
    CB = NB // P
    KS, FS = KC // CPS, FC // CPS
    QB, TAIL = QKV // NB, QKV % NB
    PC = PLE // P
    assert T == 2 and PC == CPS and KVH == 2 and CB == 4 and KS % RING == 0 and 2 * FS % RING == 0
    slope = [2.0 ** (-8.0 * (n + 1) / H) for n in range(H)]
    head_slope = slope[1::2] + slope[0::2]

    S_FFN1 = 0
    S_DOWN1 = S_FFN1 + 2 * KS * FB
    S_QKV = S_DOWN1 + NBD * FS
    S_WO = S_QKV + (QB + 1) * KS
    S_FFN2 = S_WO + NBD * KS
    S_DOWN2 = S_FFN2 + 2 * KS * FB
    S_PROJ = S_DOWN2 + NBD * FS
    S_GATE = S_PROJ + NBD
    S_END = S_GATE + NBD * KS
    QH = 3 * AW
    KB = QH + BH * HD
    VB = KB + KVH * HD
    ZK, ZQ, ZKB = AW, 2 * AW, 2 * AW + BH * HD
    ZW = ZKB + KVH * HD
    QKV_BLOCKS = [(QH, NB), (KB, TAIL), (QH + NB, NB)] + [(part * AW + half * NB, NB)
                                                          for half in range(AW // NB) for part in range(3)]
    assert len(QKV_BLOCKS) == QB + 1 and sum(w for _, w in QKV_BLOCKS) == QKV
    B_QKV = 2 * FB + NBD
    B_WO = B_QKV + QB + 1
    B_FFN2 = B_WO + NBD
    B_PROJ = B_FFN2 + 2 * FB + NBD
    B_GATE = B_PROJ + NBD
    BPB = CB // CPS
    XU = KC // CPS
    U_X1 = 0
    U_H1 = U_X1 + XU
    U_MIX = U_H1 + BPB * FB
    U_O = U_MIX + XU
    U_X2 = U_O + XU
    U_H2 = U_X2 + XU
    U_P = U_H2 + BPB * FB
    U_PLE = U_P + 1
    S_TURN_P = 12
    UW = NB // BPB
    HU = XU // 2
    O_UNITS = list(range(HU, XU)) + list(range(HU))
    J_IN1, J_POST1, J_MIX, J_OB, J_OA, J_POSTM, J_IN2, J_POST2, J_PLE, J_POSTP = range(10)
    NJOB = 10
    OBLK = AW // NB
    FACTORS = [f for j in range(NJOB)
               for f in ([(j, 0, 1), (j, 1, 2)] if j in (J_POST1, J_POSTM, J_POST2, J_POSTP) else [(j, 0, T)])]

    def factors_up_to(job, t=T - 1):
        return 1 + max(i for i, (j, _, to) in enumerate(FACTORS) if j < job or j == job and to <= max(t + 1, 1))

    squares = [T * (OBLK if j in (J_OA, J_OB) else NBD) for j in range(NJOB)]
    Q = [sum(squares[:j]) for j in range(NJOB + 1)]
    R_MIX, R_X2, R_PLE, R_OUT = (XU * k for k in range(4))
    CREDIT = 2
    HALVES = [(0, 0), (1, 0), (0, 1), (1, 1)] + [(nb, half) for nb in range(2, NBD) for half in range(2)]
    WO_SLOTS = ([(hb, k) for hb in (0, 1) for k in range(HU)] + [(hb, k) for hb in (2, 3) for k in range(HU, XU - 1)]
                + [(hb, XU - 1) for hb in (2, 3)]
                + [(hb, HU * HALVES[hb][1] + k) for hb in range(4, 2 * NBD) for k in range(HU)])
    assert len(WO_SLOTS) == NBD * KS
    HALF_FIRST = [[hb for hb, _ in WO_SLOTS].index(hb) for hb in range(2 * NBD)]
    HALF_LAST = [max(j for j, slot in enumerate(WO_SLOTS) if slot[0] == hb) for hb in range(2 * NBD)]
    PAIRS_B, PAIRS = BH // 2, H // 2
    NSLOT = (QB + 1) * KS
    L_END = NSLOT + NBD * KS
    L_KEYS = 2 * KS + 1
    L_HEAD = L_KEYS + 1
    L_PAIR = [L_KEYS - 1] + [L_HEAD + 4 * pr - 1 for pr in range(1, PAIRS)]
    COUNT_PAIR = 5
    L_COUNT = L_PAIR[COUNT_PAIR] + 2
    G_VALS = BH + AH // 2
    WEIGH_AT = [L_HEAD + 2 * h + 2 for h in range(G_VALS)] + [NSLOT + d for d in (0, 1, 3, 3, 5, 6, 8, 10)]
    PAIR_O_AT = [L_HEAD + 4 * q + 5 for q in range(G_VALS // 2)] + [NSLOT + d for d in (2, 4, 7, 11)]
    O_TURN_AT = [NSLOT - KS + 1 + k for k in range(HU)] + [NSLOT + d for d in (3, 4, 7, 12)]
    assert len(WEIGH_AT) == H and len(PAIR_O_AT) == PAIRS and len(O_TURN_AT) == XU

    def slot_width(n):
        return TAIL if isinstance(n, int) and S_QKV + KS <= n < S_QKV + 2 * KS else NB

    def rows(w):
        return w[0].rearrange("(c p) n -> p c n", p=P)

    with ExitStack() as ctx:
        where = [(nc.sbuf_base + 127) // 128 * 128]

        def sb(name, shape, dt=F32):
            size = 4 if dt != BF16 else 2
            for d in shape[1:]:
                size *= d
            t = nc.alloc_sbuf_tensor_at(name, shape, dt, offset=where[0])
            where[0] += (size + 31) // 32 * 32
            return t

        def sem(name):
            return ctx.enter_context(nc.semaphore(name))

        raw = sb("raw", [P, RING, CPS, NB])
        w_high = sb("w_high", [P, RING, CPS, NB], F32R)
        w_rest = sb("w_rest", [P, RING, CPS, NB], F32R)
        x_high = sb("x_high", [P, KC, S], F32R)
        x_rest = sb("x_rest", [P, KC, S], F32R)
        resid = sb("resid", [P, T, D])
        branch = sb("branch", [P, T, D])
        silu_g = branch[:, 0, 0:T * NB].rearrange("p (t n) -> p t n", t=T)
        hidden = branch[:, 1, 0:T * NB].rearrange("p (t n) -> p t n", t=T)
        gain_row = sb("gain_row", [P, 2, NB])
        ident = sb("ident", [P, P])
        NG = 5
        G_FFN1, G_MIX, G_O, G_FFN2, G_PLE = (KC * k for k in range(NG))
        gain_in = branch[0:(NG - 1) * KC, 0, T * NB:T * NB + P]
        gain_T = sb("gain_T", [P, NG * KC])
        junk = sb("junk", [P, 2, NB], BF16)
        stat = sb("stat", [P, NJOB, T, NBD])
        ssum = sb("ssum", [P, NJOB, T])
        msq = sb("msq", [P, NJOB, T])
        rstd = sb("rstd", [P, NJOB, T])
        minus_half = sb("minus_half", [P, T])
        sinks = sb("sinks", [P, BH])
        spare = sb("spare", [P, 4])
        turns_from = where[0]
        h_high = sb("h_high", [P, FC, S], F32R)
        h_rest = sb("h_rest", [P, FC, S], F32R)
        turns_to = where[0]
        assert turns_to <= nc.sbuf_usable_end
        where[0] = turns_from
        z = sb("z", [P, T, ZW])
        bias_row = sb("bias_row", [P, QKV])
        vals = sb("vals", [P, T, AH + KVH, VW])
        k_swap = sb("k_swap", [P, T, KVH * HD])
        kb_T = sb("kb_T", [P, 2, S])
        qk_T = sb("qk_T", [P, 2, 2, S])
        dist_i = sb("dist_i", [P, 3 * P], I32)
        bits = sb("bits", [P, 3 * P], I32)
        dist = sb("dist", [P, 3 * P])
        count = sb("count", [P, 3 * P])
        dist_a = sb("dist_a", [P, 3 * P])
        dist_b = sb("dist_b", [P, 3 * P])
        count_T = sb("count_T", [P, 3 * P])
        score = sb("score", [P, 2, 3 * P])
        prob = sb("prob", [P, 2, 3 * P])
        PTR = 4
        prob_T = sb("prob_T", [P, PTR, 3 * P])
        peak = sb("peak", [P, 2, T])
        neg_peak = sb("neg_peak", [P, 2, T])
        neg_sinks = sb("neg_sinks", [P, BH])
        sink_e = sb("sink_e", [P, BH, T])
        denom = sb("denom", [P, 2 * T])
        assert where[0] <= turns_to
        where[0] = turns_from
        p_sb = sb("p_sb", [P, T, PLE])
        assert where[0] <= turns_from + CPS * S * 4
        p_high = sb("p_high", [P, PC, S], F32R)
        p_rest = sb("p_rest", [P, PC, S], F32R)
        emb = sb("emb", [P, T, D])
        ple_row = sb("ple_row", [P, D])
        sig = sb("sig", [P, T, NB])
        gated = sb("gated", [P, T, NB])
        assert where[0] <= turns_to
        where[0] = turns_from
        gain1_in = sb("gain1_in", [KC, P])

        bank = [ctx.enter_context(nc.psum_tensor(f"bank{i}", [P, NB], F32)) for i in range(8)]
        acc = [bank[0:2], bank[2:4]]
        turn = bank[4:8]

        w_landed = [sem(f"w_landed{k}") for k in range(RING)]
        w_high_done, w_rest_done, w_used = sem("w_high_done"), sem("w_rest_done"), sem("w_used")
        tile_done = sem("tile_done")
        x_landed = [sem(f"x_landed{k}") for k in range(XU)]
        gain1_landed, gains_landed = sem("gain1_landed"), sem("gains_landed")
        sinks_landed, p_landed = sem("sinks_landed"), sem("p_landed")
        row_landed = [sem("row_landed0"), sem("row_landed1")]
        bias_landed = sem("bias_landed")
        bias_o_landed, gain_mix_landed = sem("bias_o_landed"), sem("gain_mix_landed")
        ple_row_landed, out_landed = sem("ple_row_landed"), sem("out_landed")
        pool_step, dve_step = sem("pool_step"), sem("dve_step")
        ident_ready, dist_ready = sem("ident_ready"), sem("dist_ready")
        gain_turned, gain_T_ready = sem("gain_turned"), sem("gain_T_ready")
        resid_ready = sem("resid_ready")
        turned = sem("turned")
        turn_high = sem("turn_high")
        turn_rest = sem("turn_rest")
        silu_ready, hidden_ready = sem("silu_ready"), sem("hidden_ready")
        squared, summed, rstd_ready = sem("squared"), sem("summed"), sem("rstd_ready")
        half_out = sem("half_out")
        branch_ready = sem("branch_ready")
        z_ready, ones_ready, swap_ready = sem("z_ready"), sem("ones_ready"), sem("swap_ready")
        count_ready, count_turned, count_T_ready = sem("count_ready"), sem("count_turned"), sem("count_T_ready")
        pair_turned, pair_T_ready = sem("pair_turned"), sem("pair_T_ready")
        scored, scores_read, peak_found = sem("scored"), sem("scores_read"), sem("peak_found")
        peak_ready, prob_ready, prob_turned = sem("peak_ready"), sem("prob_ready"), sem("prob_turned")
        prob_T_a, prob_T_b = sem("prob_T_a"), sem("prob_T_b")
        weighed, o_ready = sem("weighed"), sem("o_ready")
        emb_ready, sig_ready, gated_ready = sem("emb_ready"), sem("sig_ready"), sem("gated_ready")

        def wait_prob_T(eng, h):
            if h < BH:
                eng.wait_ge(prob_T_b, h + 1)
            else:
                eng.wait_ge(prob_T_a, h - BH + 1)

        pair_bank, o_bank, score_bank, prob_bank = bank[6], bank[7], bank[4], bank[5]

        def o_turn_bank(k):
            return acc[B_WO % 2][k % 2] if k < HU else pair_bank

        def blocks_for_pair(pr):
            if pr < PAIRS_B:
                return 1 if pr < PAIRS_B // 2 else 3
            return 5 if pr < (PAIRS_B + PAIRS) // 2 else 8

        def blocks_for_values(h):
            if h < BH:
                return 2
            return 6 if h < G_VALS else 9

        block = ctx.enter_context(nc.Block())

        @block.sync
        def _(sp):
            def load(n, k, src):
                if not (isinstance(n, int) and n < RING):
                    sp.wait_ge(w_rest_done, n - (RING - 1))
                sp.dma_start(raw[:, k, :, 0:src.shape[2]], src).then_inc(w_landed[k], 16)

            def load_block(n, w, slots, col, k0=0, s0=0, width=NB):
                v = rows(w)
                for s in range(s0, slots):
                    load(n + s, (k0 + s) % RING, v[:, CPS * s:CPS * s + CPS, bass.ds(col, width)])

            def ffn(n0, wg, wu, s0=0):
                load_block(n0, wg, KS, 0, s0=s0)
                load_block(n0 + KS, wu, KS, 0)
                with sp.Fori(1, FB) as i:
                    load_block(n0 + 2 * KS * i, wg, KS, NB * i)
                    load_block(n0 + KS + 2 * KS * i, wu, KS, NB * i)

            def down(n0, w, gain, blocks):
                with sp.Fori(0, NBD // 2) as j:
                    for h in range(2):
                        sp.wait_ge(branch_ready, CREDIT - 1 + blocks + 2 * j + h)
                        sp.dma_start(gain_row[:, h, :], gain[:, bass.ds(2 * NB * j + NB * h, NB)].to_broadcast([P, NB])
                                     ).then_inc(row_landed[h], 16)
                        load_block(n0 + FS * h + 2 * FS * j, w, FS, 2 * NB * j + NB * h, k0=FS * h)

            xv = x[0].rearrange("(t p) d -> p t d", p=P)
            for k in range(XU):
                sp.dma_start(resid[:, :, k * UW:(k + 1) * UW],
                             xv[:, :, k * UW:(k + 1) * UW]).then_inc(x_landed[k], 16)
                if k < RING or k % 2:
                    s = k if k < RING else RING + (k - RING) // 2
                    load(s, s % RING, rows(w_ffn1_gate)[:, CPS * s:CPS * s + CPS, 0:NB])
            ffn(S_FFN1, w_ffn1_gate, w_ffn1_up, RING + (XU - RING) // 2)
            down(S_DOWN1, w_ffn1_down, g_ffn1_post, 0)
            for i, (col, width) in enumerate(QKV_BLOCKS):
                if i == 0:
                    load_block(S_QKV, w_qkv, RING, col)
                    sp.wait_ge(w_used, S_QKV)
                    sp.dma_start(bias_row[:], b_qkv[:, :].to_broadcast([P, QKV])).then_inc(bias_landed, 16)
                load_block(S_QKV + KS * i, w_qkv, KS, col, s0=0 if i else RING, width=width)
            for j, (hb, k) in enumerate(WO_SLOTS):
                nb, c = HALVES[hb][0], CPS * O_UNITS[k]
                load(S_WO + j, j % RING, rows(w_o)[:, c:c + CPS, nb * NB:(nb + 1) * NB])
            ffn(S_FFN2, w_ffn2_gate, w_ffn2_up)
            down(S_DOWN2, w_ffn2_down, g_ffn2_post, 2 * NBD)
            for nb in range(NBD):
                load(S_PROJ + nb, nb, rows(w_ple_proj)[:, :, nb * NB:(nb + 1) * NB])
            with sp.Fori(0, NBD // 2) as j:
                for h in range(2):
                    load_block(S_GATE + KS * h + 2 * KS * j, w_ple_gate, KS, 2 * NB * j + NB * h)
            ov = out[0].rearrange("(t p) d -> p t d", p=P)
            for t in range(T):
                for nb in range(NBD):
                    sp.wait_ge(resid_ready, R_OUT + NBD * t + nb + 1)
                    sp.dma_start(ov[:, t, nb * NB:(nb + 1) * NB], resid[:, t, nb * NB:(nb + 1) * NB]
                                 ).then_inc(out_landed, 16)
            sp.wait_ge(out_landed, 16 * T * NBD)

        @block.gpsimd
        def _(pool):
            steps = [0]

            def step(ins):
                steps[0] += 1
                ins.then_inc(pool_step, 1)
                pool.wait_ge(pool_step, steps[0])

            step(nc.gpsimd.memset(ident[:], 0.0))
            nc.gpsimd.affine_select(out=ident[:], in_=ident[:], compare_op=ALU.not_equal, fill=1.0,
                                    base=0, pattern=[[-1, P]], channel_multiplier=1).then_inc(ident_ready, 1)
            step(nc.gpsimd.memset(minus_half[:], -0.5))

            done = [0]

            def factors(count):
                for job, t0, t1 in FACTORS[done[0]:count]:
                    done[0] += 1
                    pool.wait_ge(summed, done[0])
                    nc.gpsimd.tensor_tensor(rstd[:, job, t0:t1], msq[:, job, t0:t1], minus_half[:, t0:t1], ALU.pow
                                            ).then_inc(rstd_ready, 1)

            factors(factors_up_to(J_MIX))
            pool.wait_ge(w_used, S_QKV)
            nc.gpsimd.iota(dist_i[:, 0:2 * P], [[-1, 2 * P]], base=P, channel_multiplier=1).then_inc(dist_ready, 1)
            nc.gpsimd.iota(dist_i[:, 2 * P:3 * P], [[-1, P]], base=0, channel_multiplier=1).then_inc(dist_ready, 1)
            nc.gpsimd.memset(vals[:, :, :, HD:VW], 1.0).then_inc(ones_ready, 1)
            pool.wait_ge(z_ready, 2)
            for t in range(T):
                nc.gpsimd.tensor_copy(k_swap[:, t, 0:HD], z[:, t, ZKB + HD:ZKB + 2 * HD]).then_inc(swap_ready, 1)
                nc.gpsimd.tensor_copy(k_swap[:, t, HD:2 * HD], z[:, t, ZKB:ZKB + HD]).then_inc(swap_ready, 1)
            factors(len(FACTORS))

        @block.tensor
        def _(pe):
            def products(n, t, k, high, rest, chunk, o, first, last):
                width = slot_width(n)
                for c in range(CPS):
                    xh = high[:, chunk + c, t * P:(t + 1) * P]
                    xr = rest[:, chunk + c, t * P:(t + 1) * P]
                    nc.tensor.matmul(o[:, 0:width], xh, w_high[:, k, c, 0:width], start=first and c == 0, stop=False)
                    nc.tensor.matmul(o[:, 0:width], xh, w_rest[:, k, c, 0:width], start=False, stop=False)
                    ins = nc.tensor.matmul(o[:, 0:width], xr, w_high[:, k, c, 0:width], start=False,
                                           stop=last and c == CPS - 1)
                return ins

            def use_slot(n, k, high, rest, chunk, pair, first, last):
                pe.wait_ge(w_rest_done, n + 1)
                for t in range(T):
                    ins = products(n, t, k, high, rest, chunk, pair[t], first, last)
                ins.then_inc(w_used, 1)

            def use_last_slots(n, k, high, rest, chunk, pair, slots=2):
                for t in range(T):
                    for m in range(slots):
                        if t == 0:
                            pe.wait_ge(w_rest_done, n + m + 1)
                        ins = products(n + m, t, k + m, high, rest, chunk + CPS * m, pair[t], False, m == slots - 1)
                        if t == 0 and m == slots - 1:
                            ins.then_inc(tile_done, 1)
                        if t == T - 1:
                            ins.then_inc(w_used, 1)

            def turn_chunks(src, b):
                for c in range(CPS):
                    for t in range(T):
                        ins = nc.tensor.transpose(b[:, (c * T + t) * P:(c * T + t + 1) * P], src(t, c), ident[:])
                ins.then_inc(turned, 1)

            def turn_unit(src, u0, k, unit, sem_, need):
                pe.wait_ge(sem_, need)
                free = u0 + max(0, k - len(turn) + 1)
                if free:
                    pe.wait_ge(turn_rest, free)
                turn_chunks(lambda t, c: src(t, CPS * unit + c), turn[k % len(turn)])

            def lead_block(n0, b, u0, turn_k, turned_before=0):
                for k in range(turned_before, 2):
                    turn_k(k)
                for s in range(KS):
                    pe.wait_ge(turn_rest, u0 + s + 1)
                    use_slot(n0 + s, s % RING, x_high, x_rest, CPS * s, acc[b % 2], s == 0, s == KS - 1)
                    if s + 2 < KS and s + 2 >= turned_before:
                        turn_k(s + 2)

            def x_block(n0, b):
                for s in range(KS):
                    use_slot(n0 + s, s % RING, x_high, x_rest, CPS * s, acc[b % 2], s == 0, s == KS - 1)

            def resid_chunk(t, c):
                return resid[:, t, c * P:(c + 1) * P]

            def o_chunk(t, c):
                at = c * P if c < AW // P else ZQ + c * P - AW
                return z[:, t, at:at + P]

            def warm_up(times, b=bank[3]):
                for _ in range(times):
                    nc.tensor.matmul(b[:, 0:P], ident[:], ident[:], start=True, stop=True)

            def turn_x(k):
                turn_unit(resid_chunk, U_X1, k, k, x_landed[k], 16)
                if k == 0:
                    pe.wait_ge(gain1_landed, 16)
                    nc.tensor.transpose(bank[2][:, 0:KC], gain1_in[:], ident[0:KC, 0:KC]).then_inc(gain_turned, 1)
                if k < 2:
                    warm_up(WARM_2)

            def turn_x2(k):
                turn_unit(resid_chunk, U_X2, k, k, resid_ready, R_X2 + k + 1)
                if k == 1:
                    warm_up(WARM_3, acc[B_FFN2 % 2][0])

            def turn_gains():
                pe.wait_ge(gains_landed, 16 * NG)
                pe.wait_ge(turn_rest, U_X1 + XU)
                n = (NG - 1) * KC
                nc.tensor.transpose(turn[3][:, 0:n], gain_in, ident[0:n, 0:n]).then_inc(gain_turned, 1)

            def turn_hidden(i, u_h, f):
                pe.wait_ge(hidden_ready, f * FB + i)
                pe.wait_ge(turn_rest, u_h - BPB + BPB * i)
                for j in range(BPB):
                    turn_chunks(lambda t, c: hidden[:, t, (CPS * j + c) * P:(CPS * j + c + 1) * P], turn[j])

            def ffn(n0, b0, u_x, u_h, f):
                even, odd = acc[b0 % 2], acc[(b0 + 1) % 2]

                if f:
                    pe.wait_ge(half_out, T * (2 * NBD - 1))
                    warm_up(WARM_X2, even[0])
                    lead_block(n0, b0, u_x, turn_x2)
                    pe.wait_ge(half_out, T * 2 * NBD)
                else:
                    lead_block(n0, b0, u_x, turn_x)
                    pe.wait_ge(gain_T_ready, 1)
                x_block(n0 + KS, b0 + 1)
                if not f:
                    turn_gains()
                with pe.Fori(1, FB) as i:
                    n = n0 + 2 * KS * i
                    pe.wait_ge(silu_ready, f * FB + i)
                    for s in range(KS):
                        use_slot(n + s, s % RING, x_high, x_rest, CPS * s, even, s == 0, s == KS - 1)
                        if s == 1:
                            turn_hidden(i, u_h, f)
                    pe.wait_ge(hidden_ready, f * FB + i)
                    for s in range(KS):
                        use_slot(n + KS + s, s % RING, x_high, x_rest, CPS * s, odd, s == 0, s == KS - 1)
            def down(n0, b0, u_h, f):
                pe.wait_ge(silu_ready, f * FB + FB)
                for nb in range(NBD):
                    n, k0 = n0 + FS * nb, FS * nb
                    pe.wait_ge(branch_ready, CREDIT - 1 + 2 * NBD * f + nb)
                    for s in range(FS - 2 if nb == NBD - 1 else FS):
                        if nb == 0:
                            pe.wait_ge(turn_rest, u_h + s + 1)
                        use_slot(n + s, (k0 + s) % RING, h_high, h_rest, CPS * s, acc[(b0 + nb) % 2],
                                 s == 0, s == FS - 1)
                        if nb == 0 and s == 0:
                            turn_hidden(FB, u_h, f)
                        if f and nb == NBD - 1 and s == S_TURN_P:
                            turn_p()
                use_last_slots(n + FS - 2, (k0 + FS - 2) % RING, h_high, h_rest, CPS * (FS - 2),
                               acc[(b0 + NBD - 1) % 2])

            def turn_p():
                pe.wait_ge(p_landed, 16)
                turn_chunks(lambda t, c: p_sb[:, t, c * P:(c + 1) * P], turn[len(turn) - 1])

            pe.wait_ge(ident_ready, 1)
            warm_up(WARM_1)
            ffn(S_FFN1, 0, U_X1, U_H1, 0)
            down(S_DOWN1, 2 * FB, U_H1, 0)

            def turn_shared_keys():
                pe.wait_ge(z_ready, 2)
                pe.wait_ge(swap_ready, 2 * T)
                pe.wait_ge(pair_T_ready, 1)
                for t in range(T):
                    nc.tensor.transpose(pair_bank[:, t * P:(t + 1) * P], z[:, t, ZKB:ZKB + P], ident[:])
                for t in range(T):
                    ins = nc.tensor.transpose(pair_bank[:, S + t * P:S + (t + 1) * P], k_swap[:, t, :], ident[:])
                ins.then_inc(pair_turned, 1)

            def turn_pair(pr):
                pe.wait_ge(z_ready, blocks_for_pair(pr))
                if pr:
                    pe.wait_ge(pair_T_ready, pr + 1)
                else:
                    pe.wait_ge(turn_rest, U_MIX + XU)
                if pr == COUNT_PAIR + 1:
                    pe.wait_ge(count_T_ready, 1)
                if pr == PAIRS - 1:
                    pe.wait_ge(turn_rest, U_O + HU + 2)
                at = ZQ + pr * P if pr < PAIRS_B else (pr - PAIRS_B) * P
                for t in range(T):
                    ins = nc.tensor.transpose(pair_bank[:, t * P:(t + 1) * P], z[:, t, at:at + P], ident[:])
                if pr >= PAIRS_B:
                    for t in range(T):
                        ins = nc.tensor.transpose(pair_bank[:, S + t * P:S + (t + 1) * P],
                                                  z[:, t, ZK + at:ZK + at + P], ident[:])
                ins.then_inc(pair_turned, 1)

            def turn_count():
                pe.wait_ge(count_ready, 1)
                pe.wait_ge(pair_T_ready, COUNT_PAIR + 2)
                for c in range(3):
                    ins = nc.tensor.transpose(pair_bank[:, c * P:(c + 1) * P], count[:, c * P:(c + 1) * P], ident[:])
                ins.then_inc(count_turned, 1)

            def scores(g):
                pe.wait_ge(pair_T_ready, g // 2 + 2)
                if g:
                    pe.wait_ge(scores_read, g)
                lo = HD * (g % 2)
                q = qk_T[lo:lo + HD, (g // 2) % 2, 0, :]
                if g < BH:
                    k = kb_T[lo:lo + HD, (g // (BH // KVH) + g) % 2, :]
                else:
                    k = qk_T[lo:lo + HD, (g // 2) % 2, 1, :]
                b = score_bank
                nc.tensor.matmul(b[:, 0:S], q[:, P:S], k, start=True, stop=True)
                nc.tensor.matmul(b[:, S:S + P], q[:, 0:P], k[:, 0:P], start=True, stop=True).then_inc(scored, 1)

            def turn_prob(h):
                pe.wait_ge(prob_ready, h + 1)
                if h:
                    wait_prob_T(pe, h - 1)
                for c in range(3):
                    ins = nc.tensor.transpose(prob_bank[:, c * P:(c + 1) * P],
                                              prob[:, h % 2, c * P:(c + 1) * P], ident[:])
                ins.then_inc(prob_turned, 1)

            def weigh(h):
                wait_prob_T(pe, h)
                pe.wait_ge(z_ready, blocks_for_values(h))
                pe.wait_ge(ones_ready, 1)
                if h % 2 == 0 and h:
                    pe.wait_ge(o_ready, h // 2)
                v = AH + h // (BH // KVH) if h < BH else h - BH
                w = prob_T[:, h % PTR, :]
                o = [o_bank[:, (h % 2 * T + t) * VW:(h % 2 * T + t + 1) * VW] for t in range(T)]
                nc.tensor.matmul(o[1], w[:, 0:P], vals[:, 0, v, :], start=True, stop=False)
                nc.tensor.matmul(o[1], w[:, P:2 * P], vals[:, 1, v, :], start=False, stop=True)
                nc.tensor.matmul(o[0], w[:, 2 * P:3 * P], vals[:, 0, v, :], start=True, stop=True
                                 ).then_inc(weighed, 1)

            def turn_mix(k):
                turn_unit(resid_chunk, U_MIX, k, k, resid_ready, R_MIX + k + 1)

            def turn_o(k):
                pe.wait_ge(o_ready, 2 * (k + 1))
                if k < 2:
                    pe.wait_ge(z_ready, QB)
                elif k < HU:
                    pe.wait_ge(turn_rest, U_O + k - 1)
                elif k == HU:
                    pe.wait_ge(pair_T_ready, PAIRS)
                elif k == HU + 2:
                    pe.wait_ge(pair_T_ready, PAIRS + 1)
                else:
                    pe.wait_ge(turn_rest, U_O + k)
                turn_chunks(lambda t, c: o_chunk(t, CPS * O_UNITS[k] + c), o_turn_bank(k))

            pe.wait_ge(branch_ready, CREDIT + NBD - 1)
            warm_up(WARM_MIX, acc[B_QKV % 2][0])
            turn_mix(0)
            turn_mix(1)
            warm_up(WARM_3, acc[B_QKV % 2][0])
            for L in range(L_END):
                if L < NSLOT:
                    i, s = divmod(L, KS)
                    if i == 0:
                        pe.wait_ge(turn_rest, U_MIX + s + 1)
                    if i >= 2 and s == 0:
                        pe.wait_ge(z_ready, i - 1)
                    use_slot(S_QKV + L, s % RING, x_high, x_rest, CPS * s, acc[(B_QKV + i) % 2], s == 0, s == KS - 1)
                else:
                    j = L - NSLOT
                    hb, k = WO_SLOTS[j]
                    if j == HALF_FIRST[hb]:
                        if hb == 0:
                            pe.wait_ge(turn_rest, U_O + HU)
                        elif hb == 1:
                            pe.wait_ge(z_ready, QB + 1)
                        else:
                            pe.wait_ge(half_out, T * (hb - 1))
                    pe.wait_ge(turn_rest, U_O + k + 1)
                    if L == L_END - 2:
                        use_last_slots(S_QKV + L, j % RING, x_high, x_rest, CPS * k, acc[(B_WO + hb) % 2])
                    if L >= L_END - 2:
                        continue
                    use_slot(S_QKV + L, j % RING, x_high, x_rest, CPS * k, acc[(B_WO + hb) % 2],
                             j == HALF_FIRST[hb], j == HALF_LAST[hb])
                if L + 2 < XU:
                    turn_mix(L + 2)
                if L == L_KEYS:
                    turn_shared_keys()
                for h in range(H):
                    if L == WEIGH_AT[h]:
                        weigh(h)
                    if L == L_HEAD + 2 * h:
                        scores(h)
                    if L == L_HEAD + 2 * h + 1:
                        turn_prob(h)
                for pr in range(PAIRS):
                    if L == L_PAIR[pr]:
                        turn_pair(pr)
                if L == L_COUNT:
                    turn_count()
                for k in range(XU):
                    if L == O_TURN_AT[k]:
                        turn_o(k)
            ffn(S_FFN2, B_FFN2, U_X2, U_H2, 1)
            down(S_DOWN2, B_FFN2 + 2 * FB, U_H2, 1)
            def turn_ple(k):
                turn_unit(resid_chunk, U_PLE, k, k, resid_ready, R_PLE + k + 1)

            pe.wait_ge(turn_rest, U_PLE)
            for nb in range(NBD):
                if nb < 2:
                    pe.wait_ge(branch_ready, CREDIT + 3 * NBD - 1 + nb)
                else:
                    pe.wait_ge(emb_ready, nb - 1)
                use_slot(S_PROJ + nb, nb, p_high, p_rest, 0, acc[(B_PROJ + nb) % 2], True, True)
                if nb >= 2:
                    turn_ple(nb - 2)
            pe.wait_ge(emb_ready, NBD - 1)
            lead_block(S_GATE, B_GATE, U_PLE, turn_ple, turned_before=2)
            for nb in range(1, NBD):
                if nb == 1:
                    pe.wait_ge(emb_ready, NBD)
                else:
                    pe.wait_ge(sig_ready, T * (nb - 1))
                for s in range(KS - RING if nb == NBD - 1 else KS):
                    use_slot(S_GATE + KS * nb + s, s % RING, x_high, x_rest, CPS * s, acc[(B_GATE + nb) % 2],
                             s == 0, s == KS - 1)
            use_last_slots(S_END - RING, 0, x_high, x_rest, CPS * (KS - RING), acc[(B_GATE + NBD - 1) % 2], RING)

        @block.scalar
        def _(act):
            def high(n, k):
                if isinstance(n, int) and n >= S_END:
                    return
                act.wait_ge(w_landed[k], 4 * n - 4 * k + 16)
                if not (isinstance(n, int) and n < RING):
                    act.wait_ge(w_used, n - (RING - 1))
                width = slot_width(n)
                nc.scalar.copy(w_high[:, k, :, 0:width], raw[:, k, :, 0:width]).then_inc(w_high_done, 1)

            def ahead(n, s0, count_, k0=0):
                for s in range(s0, s0 + count_):
                    high(n + s + RING, (k0 + s) % RING)

            def square(q, src, job, t, b):
                if not (isinstance(q, int) and q < 2):
                    act.wait_ge(squared, q - 1)
                nc.scalar.activation(junk[:, t % 2, :], src, ACT.Square, accum_out=stat[:, job, t, b]
                                     ).then_inc(squared, 1)

            def col(b):
                return slice(b, b + 1)

            def blk(b):
                return slice(b * NB, (b + 1) * NB)

            def x_unit(u0, k, gain, b=None):
                b = b or turn[k % len(turn)]
                act.wait_ge(turned, u0 + k + 1)
                for c in range(CPS):
                    ins = nc.scalar.activation(x_high[:, CPS * k + c, :], b[:, c * S:(c + 1) * S], ACT.Copy,
                                               scale=gain_T[:, gain + c:gain + c + 1])
                ins.then_inc(turn_high, 1)

            def square_resid(job, nb):
                for t in range(T):
                    square(Q[job] + T * nb + t, resid[:, t, blk(nb)], job, t, col(nb))

            def boundary(u0, gain, n0, job):
                act.wait_ge(gain_T_ready, 2)
                for k in range(XU):
                    x_unit(u0, k, gain + CPS * k)
                    if k in (1, 2):
                        high(n0 + k + 1, k + 1)
                    if k >= RING:
                        high(n0 + k, k % RING)
                    if k % BPB == 1:
                        square_resid(job, k // BPB)

            def ffn(n0, b0, u_h, job):
                def silu(i):
                    act.wait_ge(w_used, n0 + KS + 2 * KS * i)
                    for t in range(T):
                        ins = nc.scalar.activation(silu_g[:, t, :], acc[b0 % 2][t][:], ACT.Silu,
                                                   scale=rstd[:, job, t:t + 1])
                    ins.then_inc(silu_ready, 1)

                def hidden_high(i):
                    for j in range(BPB):
                        act.wait_ge(turned, u_h - BPB + j + 1 + BPB * i)
                        nc.scalar.copy(h_high[:, bass.ds(CB * i - CB + CPS * j, CPS), :],
                                       turn[j][:].rearrange("p (c s) -> p c s", c=CPS)).then_inc(turn_high, 1)

                ahead(n0, KS - RING, RING - 1)
                act.wait_ge(rstd_ready, factors_up_to(job))
                silu(0)
                ahead(n0, KS - 1, KS + 1)
                with act.Fori(1, FB) as i:
                    n = n0 + 2 * KS * i
                    ahead(n, 0, 3)
                    hidden_high(i)
                    ahead(n, 3, KS - 4)
                    silu(i)
                    ahead(n, KS - 1, KS + 1)
                hidden_high(FB)

            def down(n0, b0, job, f):
                for nb in range(NBD):
                    n, k0, pair = n0 + FS * nb, FS * nb, acc[(b0 + nb) % 2]
                    if nb < NBD - 1:
                        ahead(n, 0, FS - 1, k0)
                        act.wait_ge(w_used, n + FS)
                        for t in range(T):
                            square(Q[job] + T * nb + t, pair[t][:], job, t, col(nb))
                        ahead(n, FS - 1, 1, k0)
                        continue
                    ahead(n, 0, 1, k0)
                    if f:
                        act.wait_ge(w_used, n + 1)
                        act.dma_start(p_sb[:], p[0, 0].rearrange("(t p) e -> p t e", p=P)).then_inc(p_landed, 16)
                    ahead(n, 1, S_TURN_P, k0)
                    if f:
                        act.wait_ge(turned, U_P + 1)
                        nc.scalar.copy(p_high[:].rearrange("p c s -> p (c s)"), turn[len(turn) - 1][:]
                                       ).then_inc(turn_high, 1)
                    ahead(n, S_TURN_P + 1, FS - 3 - S_TURN_P, k0)
                    act.wait_ge(tile_done, 2 * f + 1)
                    square(Q[job] + T * nb, pair[0][:], job, 0, col(nb))
                    act.wait_ge(w_used, n + FS)
                    square(Q[job] + T * nb + 1, pair[1][:], job, 1, col(nb))

            act.dma_start(gain1_in[:], g_ffn1_pre[0].rearrange("(c p) -> c p", p=P)).then_inc(gain1_landed, 16)
            act.wait_ge(ident_ready, 1)
            nc.scalar.activation(spare[:, 2:3], ident[:, 0:1], ACT.Silu)
            act.wait_ge(gain_T_ready, 1)
            for k in range(XU):
                x_unit(U_X1, k, G_FFN1 + CPS * k)
                high(k, k % RING)
                if k % BPB == 1:
                    square_resid(J_IN1, k // BPB)
            for n, g in enumerate((g_mix_pre, None, g_ffn2_pre, g_ple_pre)):
                for src, at in [(g_out_a, 0), (g_out_b, AW // P)] if g is None else [(g, 0)]:
                    v = src[0].rearrange("(c p) -> c p", p=P)
                    act.dma_start(gain_in[n * KC + at:n * KC + at + v.shape[0], :], v).then_inc(gains_landed, 16)
            act.dma_start(sinks[:], attn_sinks.rearrange("a k g -> a (k g)").to_broadcast([P, BH])
                          ).then_inc(sinks_landed, 16)
            ffn(S_FFN1, 0, U_H1, J_IN1)
            down(S_DOWN1, 2 * FB, J_POST1, 0)
            boundary(U_MIX, G_MIX, S_QKV, J_MIX)

            def pair_out(pr):
                act.wait_ge(pair_turned, pr + 2 if pr else 1)
                if pr >= 2:
                    act.wait_ge(scored, 2 * pr - 2)
                n = 1 if pr < PAIRS_B else 2
                nc.scalar.copy(qk_T[:, pr % 2, 0:n, :], pair_bank[:, 0:n * S].rearrange("p (n s) -> p n s", n=n)
                               ).then_inc(pair_T_ready, 1)

            def exps(g):
                act.wait_ge(peak_ready, g + 1)
                if g >= 2:
                    act.wait_ge(prob_turned, g - 1)
                nc.scalar.activation(prob[:, g % 2, 0:S], score[:, g % 2, 0:S], ACT.Exp,
                                     bias=neg_peak[:, g % 2, 1:2], scale=HD ** -0.5)
                if g < BH:
                    nc.scalar.activation(sink_e[:, g, :], neg_peak[:, g % 2, :], ACT.Exp, bias=sinks[:, g:g + 1])
                nc.scalar.activation(prob[:, g % 2, S:S + P], score[:, g % 2, S:S + P], ACT.Exp,
                                     bias=neg_peak[:, g % 2, 0:1], scale=HD ** -0.5).then_inc(prob_ready, 1)

            def prob_T_out(h):
                act.wait_ge(prob_turned, h + 1)
                if h >= PTR:
                    act.wait_ge(weighed, h - PTR + 1)
                nc.scalar.copy(prob_T[:, h % PTR, :], prob_bank[:, 0:3 * P]).then_inc(prob_T_b, 1)

            def square_o(job, b, t):
                at = (ZQ if job == J_OB else 0) + b * NB
                square(Q[job] + T * b + t, z[:, t, at:at + NB], job, t, col(b))

            act.wait_ge(sinks_landed, 16)
            for L in range(L_END):
                if KS - RING <= L < L_END - 2:
                    high(S_QKV + L + RING, L % RING)
                if L == NSLOT:
                    act.wait_ge(z_ready, QB + 1)
                    act.dma_start(bias_row[:, 0:D], b_o[:, :].to_broadcast([P, D])).then_inc(bias_o_landed, 16)
                if L == NSLOT + RING:
                    act.dma_start(bias_row[:, D:2 * D], g_mix_post[:, :].to_broadcast([P, D])
                                  ).then_inc(gain_mix_landed, 16)
                if L == L_KEYS:
                    act.wait_ge(pair_turned, 2)
                    nc.scalar.copy(kb_T[:].rearrange("p a s -> p (a s)"), pair_bank[:]).then_inc(pair_T_ready, 1)
                for h in range(H):
                    if L == L_HEAD + 2 * h:
                        exps(h)
                    if L == L_HEAD + 2 * h + 1 and h < BH:
                        prob_T_out(h)
                for pr in range(PAIRS):
                    if L == L_PAIR[pr]:
                        pair_out(pr)
                for k in range(XU):
                    if L == O_TURN_AT[k]:
                        x_unit(U_O, k, G_O + CPS * O_UNITS[k], o_turn_bank(k))
                for m in range(T * OBLK):
                    if L == PAIR_O_AT[PAIRS_B - 1] + 2 + 2 * m:
                        act.wait_ge(o_ready, PAIRS_B)
                        square_o(J_OB, m // T, m % T)
                if L == PAIR_O_AT[G_VALS // 2 - 1] + 3:
                    act.wait_ge(o_ready, G_VALS // 2)
                    for t in range(T):
                        square_o(J_OA, 0, t)
                if L == PAIR_O_AT[PAIRS - 1]:
                    act.wait_ge(o_ready, PAIRS)
                    for t in range(T):
                        square_o(J_OA, 1, t)
                for hb, (nb, half) in enumerate(HALVES):
                    if half and L == NSLOT + HALF_LAST[hb]:
                        for t in range(T):
                            act.wait_ge(half_out, T * hb + t + 1)
                            square(Q[J_POSTM] + T * nb + t, branch[:, t, blk(nb)], J_POSTM, t, col(nb))
            boundary(U_X2, G_FFN2, S_FFN2, J_IN2)
            ffn(S_FFN2, B_FFN2, U_H2, J_IN2)
            down(S_DOWN2, B_FFN2 + 2 * FB, J_POST2, 1)
            act.dma_start(ple_row[:], g_ple_post[:, :].to_broadcast([P, D])).then_inc(ple_row_landed, 16)
            high(S_PROJ + 2, 2)
            high(S_PROJ + 3, 3)
            for nb in range(NBD):
                act.wait_ge(w_used, S_PROJ + nb + 1)
                for t in range(T):
                    ins = nc.scalar.copy(emb[:, t, blk(nb)], acc[(B_PROJ + nb) % 2][t][:])
                ins.then_inc(emb_ready, 1)
                high(S_GATE + nb, nb)
                if nb >= 2:
                    x_unit(U_PLE, nb - 2, G_PLE + CPS * (nb - 2))
            for k in range(2, XU):
                x_unit(U_PLE, k, G_PLE + CPS * k)
                if k >= RING:
                    high(S_GATE + k, k % RING)
                if k == 2:
                    square_resid(J_PLE, 0)
                if k % BPB == 1:
                    square_resid(J_PLE, k // BPB)
            for nb in range(NBD):
                n = S_GATE + KS * nb
                ahead(n, 0 if nb else KS - RING, KS - 1 if nb else RING - 1)
                act.wait_ge(rstd_ready, factors_up_to(J_PLE))
                if nb:
                    act.wait_ge(gated_ready, T * nb)

                def gate_out(t):
                    nc.scalar.activation(sig[:, t, :], acc[(B_GATE + nb) % 2][t][:], ACT.Sigmoid,
                                         scale=rstd[:, J_PLE, t:t + 1]).then_inc(sig_ready, 1)

                def square_gated(t):
                    act.wait_ge(gated_ready, T * nb + t + 1)
                    square(Q[J_POSTP] + T * nb + t, gated[:, t, :], J_POSTP, t, col(nb))

                if nb == NBD - 1:
                    act.wait_ge(tile_done, 4)
                    gate_out(0)
                    square_gated(0)
                    act.wait_ge(w_used, S_END)
                    gate_out(1)
                    square_gated(1)
                else:
                    act.wait_ge(w_used, n + KS)
                    for t in range(T):
                        gate_out(t)
                    ahead(n, KS - 1, 1)
                    for t in range(T):
                        square_gated(t)

        @block.vector
        def _(dve):
            steps = [0]

            def step(ins):
                steps[0] += 1
                ins.then_inc(dve_step, 1)
                dve.wait_ge(dve_step, steps[0])

            def rest(n, k):
                if isinstance(n, int) and n >= S_END:
                    return
                dve.wait_ge(w_high_done, n + 1)
                width = slot_width(n)
                nc.vector.tensor_tensor(w_rest[:, k, :, 0:width], raw[:, k, :, 0:width],
                                        w_high[:, k, :, 0:width].bitcast(F32), ALU.subtract).then_inc(w_rest_done, 1)

            def ahead(n, s0, count_, k0=0):
                for s in range(s0, s0 + count_):
                    rest(n + s + RING, (k0 + s) % RING)

            def blk(b):
                return slice(b * NB, (b + 1) * NB)

            def sum_up(job, t0=0, t1=T):
                by = 4.0 if job in (J_POST1, J_POST2) else 1.0
                width = AW if job in (J_OA, J_OB) else D
                n = squares[job] // T
                dve.wait_ge(squared, Q[job + 1] - T + t1)
                step(nc.vector.reduce_sum(ssum[:, job, t0:t1], stat[:, job, t0:t1, 0:n], axis=AX.X))
                nc.vector.tensor_scalar(msq[:, job, t0:t1], ssum[:, job, t0:t1], by / width, by * EPS,
                                        ALU.mult, ALU.add).then_inc(summed, 1)

            def x_rest_unit(u0, k, gain, b=None):
                b = b or turn[k % len(turn)]
                dve.wait_ge(turn_high, u0 + k + 1)
                for c in range(CPS):
                    ins = nc.vector.scalar_tensor_tensor(
                        out=x_rest[:, CPS * k + c, :], in0=b[:, c * S:(c + 1) * S],
                        scalar=gain_T[:, gain + c:gain + c + 1], in1=x_high[:, CPS * k + c, :].bitcast(F32),
                        op0=ALU.mult, op1=ALU.subtract)
                ins.then_inc(turn_rest, 1)

            def add_branch(job, k, t):
                at = slice(k * UW, (k + 1) * UW)
                ins = nc.vector.scalar_tensor_tensor(out=resid[:, t, at], in0=branch[:, t, at],
                                                     scalar=rstd[:, job, t:t + 1], in1=resid[:, t, at],
                                                     op0=ALU.mult, op1=ALU.add)
                if t == T - 1:
                    ins.then_inc(resid_ready, 1)

            def finish_branch(job, blocks, early, times_gain, acc_out=None):
                for t in range(T):
                    if acc_out:
                        acc_out(t)
                    if t:
                        dve.wait_ge(rstd_ready, factors_up_to(job, 0))
                        for k in range(early):
                            add_branch(job, k, 0)
                    sum_up(job, t, t + 1)
                    ins = times_gain(t)
                    if t == 0:
                        step(ins)
                        dve.wait_ge(branch_ready, CREDIT + blocks - 1)
                    else:
                        ins.then_inc(branch_ready, 1)
                        dve.wait_ge(branch_ready, CREDIT + blocks)
                dve.wait_ge(rstd_ready, factors_up_to(job))
                add_branch(job, 0, T - 1)

            def update(job, k, early):
                for t in range(T):
                    if t or k >= early:
                        add_branch(job, k, t)

            def boundary(u0, gain, n0, job, early):
                for k in range(XU):
                    if k + 1 < XU:
                        update(job, k + 1, early)
                    x_rest_unit(u0, k, gain + CPS * k)
                    if k in (1, 2):
                        rest(n0 + k + 1, k + 1)
                    if k >= RING:
                        rest(n0 + k, k % RING)

            def ffn(n0, b0, u_h, job, f):
                def gate_up(i):
                    dve.wait_ge(w_used, n0 + 2 * KS + 2 * KS * i)
                    dve.wait_ge(silu_ready, f * FB + 1 + i)
                    for t in range(T):
                        ins = nc.vector.scalar_tensor_tensor(out=hidden[:, t, :], in0=acc[(b0 + 1) % 2][t][:],
                                                             scalar=rstd[:, job, t:t + 1], in1=silu_g[:, t, :],
                                                             op0=ALU.mult, op1=ALU.mult)
                    ins.then_inc(hidden_ready, 1)

                def hidden_rest(i):
                    for j in range(BPB):
                        chunks = bass.ds(CB * i - CB + CPS * j, CPS)
                        dve.wait_ge(turn_high, u_h - BPB + j + 1 + BPB * i)
                        nc.vector.tensor_tensor(h_rest[:, chunks, :], turn[j][:].rearrange("p (c s) -> p c s", c=CPS),
                                                h_high[:, chunks, :].bitcast(F32), ALU.subtract).then_inc(turn_rest, 1)

                ahead(n0, KS - RING, KS + RING - 1)
                dve.wait_ge(rstd_ready, factors_up_to(job))
                gate_up(0)
                if not f:
                    dve.wait_ge(gain_turned, 2)
                    nc.vector.tensor_copy(gain_T[:, KC:NG * KC], turn[3][:, 0:(NG - 1) * KC]).then_inc(gain_T_ready, 1)
                ahead(n0, 2 * KS - 1, 1)
                with dve.Fori(1, FB) as i:
                    n = n0 + 2 * KS * i
                    ahead(n, 0, 3)
                    hidden_rest(i)
                    ahead(n, 3, 2 * KS - 4)
                    gate_up(i)
                    ahead(n, 2 * KS - 1, 1)
                hidden_rest(FB)

            def down(n0, b0, job, f):
                def times_gain(nb, t):
                    return nc.vector.tensor_tensor(branch[:, t, blk(nb)], acc[(b0 + nb) % 2][t][:],
                                                   gain_row[:, nb % 2, :], ALU.mult)

                for nb in range(NBD):
                    n = n0 + FS * nb
                    if nb < NBD - 1:
                        ahead(n, 0, FS - 1, FS * nb)
                        dve.wait_ge(row_landed[nb % 2], 16 * (2 * f + nb // 2 + 1))
                        for t in range(T):
                            dve.wait_ge(squared, Q[job] + T * nb + t + 1)
                            ins = times_gain(nb, t)
                        ins.then_inc(branch_ready, 1)
                        ahead(n, FS - 1, 1, FS * nb)
                        continue
                    ahead(n, 0, S_TURN_P + 1, FS * nb)
                    if f:
                        dve.wait_ge(turn_high, U_P + 1)
                        nc.vector.tensor_tensor(p_rest[:].rearrange("p c s -> p (c s)"), turn[len(turn) - 1][:],
                                                p_high[:].rearrange("p c s -> p (c s)").bitcast(F32), ALU.subtract
                                                ).then_inc(turn_rest, 1)
                    ahead(n, S_TURN_P + 1, FS - 3 - S_TURN_P, FS * nb)
                    dve.wait_ge(row_landed[nb % 2], 16 * (2 * f + nb // 2 + 1))
                    finish_branch(job, (2 * f + 1) * NBD, EARLY, lambda t: times_gain(NBD - 1, t))

            nc.vector.memset(spare[:, 0:1], 0.0).then_inc(branch_ready, CREDIT)
            dve.wait_ge(gain_turned, 1)
            nc.vector.tensor_copy(gain_T[:, 0:KC], bank[2][:, 0:KC]).then_inc(gain_T_ready, 1)
            dve.wait_ge(gain_T_ready, 1)
            for k in range(XU):
                x_rest_unit(U_X1, k, G_FFN1 + CPS * k)
                rest(k, k % RING)
            sum_up(J_IN1)
            ffn(S_FFN1, 0, U_H1, J_IN1, 0)
            down(S_DOWN1, 2 * FB, J_POST1, 0)
            boundary(U_MIX, G_MIX, S_QKV, J_POST1, EARLY)
            sum_up(J_MIX)

            def project_out(i):
                col, width = QKV_BLOCKS[i]
                dve.wait_ge(w_used, S_QKV + KS * (i + 1))
                if col < 2 * AW:
                    parts = [(0, width, col, None)]
                elif col < QH:
                    parts = [(0, width, None, (col - 2 * AW) // HD)]
                elif col < KB:
                    parts = [(0, width, ZQ + col - QH, None)]
                else:
                    parts = [(0, VB - KB, ZKB, None), (VB - KB, width, None, AH)]
                for at, to, dst, head in parts:
                    for t in range(T):
                        src, b = acc[(B_QKV + i) % 2][t][:, at:to], bias_row[:, col + at:col + to]
                        if head is None:
                            o = z[:, t, dst:dst + to - at]
                        else:
                            o = vals[:, t, head:head + (to - at) // HD, 0:HD]
                            src = src.rearrange("p (h d) -> p h d", d=HD)
                            b = b.rearrange("p (h d) -> p h d", d=HD)
                        ins = nc.vector.scalar_tensor_tensor(out=o, in0=src, scalar=rstd[:, J_MIX, t:t + 1], in1=b,
                                                             op0=ALU.mult, op1=ALU.add)
                ins.then_inc(z_ready, 1)

            def table_b():
                dve.wait_ge(dist_ready, 2)
                step(nc.vector.tensor_copy(dist[:], dist_i[:]))
                step(nc.vector.tensor_scalar(dist_b[:], dist[:], 0.0, BIG, ALU.is_lt, ALU.mult))
                step(nc.vector.tensor_scalar(count[:], dist[:], float(P), BIG, ALU.is_ge, ALU.mult))
                step(nc.vector.tensor_tensor(dist_b[:], dist_b[:], count[:], ALU.add))
                step(nc.vector.tensor_tensor(dist_b[:], dist_b[:], dist[:], ALU.add))
                dve.wait_ge(sinks_landed, 16)
                step(nc.vector.tensor_scalar(neg_sinks[:], sinks[:], -1.0, None, ALU.mult))

            def table_near():
                step(nc.vector.tensor_scalar(count[:], dist[:], float(P), None, ALU.is_le))

            def table_dilated(dil):
                step(nc.vector.tensor_scalar(bits[:], dist_i[:], dil - 1, None, ALU.bitwise_and))
                step(nc.vector.tensor_copy(dist_a[:], bits[:]))
                step(nc.vector.scalar_tensor_tensor(out=count[:], in0=dist_a[:], scalar=0.0, in1=count[:],
                                                    op0=ALU.is_equal, op1=ALU.add))

            def table_count():
                nc.vector.scalar_tensor_tensor(out=count[:], in0=dist[:], scalar=0.0, in1=count[:],
                                               op0=ALU.is_ge, op1=ALU.mult).then_inc(count_ready, 1)
                dve.wait_ge(count_ready, 1)

            def table_a():
                step(nc.vector.tensor_scalar(dist_a[:], count[:], 0.0, BIG, ALU.is_equal, ALU.mult))
                step(nc.vector.tensor_tensor(dist_a[:], dist_a[:], dist[:], ALU.add))

            def soften(g):
                dve.wait_ge(scored, g + 1)
                if g >= 2:
                    dve.wait_ge(prob_ready, g - 1)
                nc.vector.scalar_tensor_tensor(out=score[:, g % 2, :], in0=(dist_b if g < BH else dist_a)[:],
                                               scalar=-head_slope[g] * HD ** 0.5, in1=score_bank[:, 0:3 * P],
                                               op0=ALU.mult, op1=ALU.add).then_inc(scores_read, 1)
                dve.wait_ge(scores_read, g + 1)
                nc.vector.reduce_max(peak[:, g % 2, 1:2], score[:, g % 2, 0:S], axis=AX.X)
                nc.vector.reduce_max(peak[:, g % 2, 0:1], score[:, g % 2, S:S + P], axis=AX.X
                                     ).then_inc(peak_found, 1)
                dve.wait_ge(peak_found, g + 1)
                if g < BH:
                    ins = nc.vector.tensor_scalar(neg_peak[:, g % 2, :], peak[:, g % 2, :], -HD ** -0.5,
                                                  neg_sinks[:, g:g + 1], ALU.mult, ALU.min)
                else:
                    ins = nc.vector.tensor_scalar(neg_peak[:, g % 2, :], peak[:, g % 2, :], -HD ** -0.5, None, ALU.mult)
                ins.then_inc(peak_ready, 1)

            def prob_T_out(h):
                dve.wait_ge(prob_turned, h + 1)
                dve.wait_ge(weighed, h - PTR + 1)
                nc.vector.tensor_tensor(prob_T[:, h % PTR, :], prob_bank[:, 0:3 * P], count_T[:], ALU.mult
                                        ).then_inc(prob_T_a, 1)

            def pair_o(q):
                dve.wait_ge(weighed, 2 * (q + 1))
                o = o_bank[:, 0:2 * T * VW].rearrange("p (n c) -> p n c", c=VW)
                if q < PAIRS_B:
                    step(nc.vector.tensor_tensor(denom[:], o[:, :, HD],
                                                 sink_e[:, 2 * q:2 * q + 2, :].rearrange("p h t -> p (h t)"), ALU.add))
                    step(nc.vector.reciprocal(denom[:], denom[:]))
                    at = ZQ + q * P
                else:
                    step(nc.vector.reciprocal(denom[:], o[:, :, HD]))
                    at = (q - PAIRS_B) * P
                o4 = o_bank[:, 0:2 * T * VW].rearrange("p (h t c) -> p h t c", h=2, t=T)
                nc.vector.tensor_tensor(
                    z[:, :, at:at + P].rearrange("p t (h d) -> p h t d", h=2), o4[:, :, :, 0:HD],
                    denom[:].rearrange("p (h t) -> p h t", h=2).unsqueeze(3).to_broadcast([P, 2, T, HD]), ALU.mult
                    ).then_inc(o_ready, 1)

            def half_block_out(hb, only=None):
                nb, half = HALVES[hb]
                if only is None:
                    dve.wait_ge(w_used, S_WO + HALF_LAST[hb] + 1)
                if half == 0:
                    dve.wait_ge(rstd_ready, factors_up_to(J_OB))
                    dve.wait_ge(bias_o_landed, 16)
                else:
                    dve.wait_ge(rstd_ready, factors_up_to(J_OA))
                    dve.wait_ge(half_out, T * (HALVES.index((nb, 0)) + 1))
                for t in range(T):
                    if hb == 2 * NBD - 1:
                        if t != only:
                            continue
                        if t == 0:
                            dve.wait_ge(tile_done, 2)
                        else:
                            dve.wait_ge(w_used, S_WO + HALF_LAST[hb] + 1)
                    nc.vector.scalar_tensor_tensor(
                        out=branch[:, t, blk(nb)], in0=acc[(B_WO + hb) % 2][t][:],
                        scalar=rstd[:, J_OA if half else J_OB, t:t + 1],
                        in1=branch[:, t, blk(nb)] if half else bias_row[:, blk(nb)],
                        op0=ALU.mult, op1=ALU.add).then_inc(half_out, 1)

            def times_gain_mix(nb, t):
                dve.wait_ge(squared, Q[J_POSTM] + T * nb + t + 1)
                return nc.vector.tensor_tensor(branch[:, t, blk(nb)], branch[:, t, blk(nb)],
                                               bias_row[:, D + nb * NB:D + (nb + 1) * NB], ALU.mult)

            for L in range(L_END):
                i, s = divmod(L, KS)
                for h in range(H):
                    if L == L_HEAD + 2 * h:
                        soften(h)
                for q in range(PAIRS):
                    if L == PAIR_O_AT[q]:
                        pair_o(q)
                for h in range(BH, H):
                    if L == L_HEAD + 2 * h + 1:
                        prob_T_out(h)
                if L == KS:
                    table_b()
                if L == L_HEAD + 1:
                    table_near()
                if L == L_HEAD + 5:
                    table_dilated(4)
                if L == L_HEAD + 9:
                    table_dilated(16)
                if L == L_HEAD + 13:
                    table_count()
                if L == L_HEAD + 17:
                    table_a()
                if L == L_COUNT:
                    dve.wait_ge(count_turned, 1)
                    step(nc.vector.tensor_copy(count_T[:], pair_bank[:, 0:3 * P]))
                    nc.vector.memset(spare[:, 1:2], 0.0).then_inc(count_T_ready, 1)
                if L == PAIR_O_AT[PAIRS_B - 1] + 4 + 2 * T * OBLK:
                    sum_up(J_OB)
                if L == PAIR_O_AT[PAIRS - 1] + 2:
                    sum_up(J_OA)
                if L < NSLOT and s == KS - 1:
                    if i == 0:
                        dve.wait_ge(rstd_ready, factors_up_to(J_MIX))
                        dve.wait_ge(bias_landed, 16)
                    project_out(i)
                for hb in range(2 * NBD - 1):
                    if L == NSLOT + HALF_LAST[hb]:
                        half_block_out(hb)
                for hb, (nb, half) in enumerate(HALVES):
                    if half and nb < NBD - 1 and L == NSLOT + HALF_LAST[hb] + 3:
                        dve.wait_ge(gain_mix_landed, 16)
                        for t in range(T):
                            ins = times_gain_mix(nb, t)
                        ins.then_inc(branch_ready, 1)
                if KS - RING <= L < L_END - 2:
                    rest(S_QKV + L + RING, s % RING)
                for k in range(XU):
                    if L == O_TURN_AT[k]:
                        x_rest_unit(U_O, k, G_O + CPS * O_UNITS[k], o_turn_bank(k))
            finish_branch(J_POSTM, 2 * NBD, EARLY_MIX, lambda t: times_gain_mix(NBD - 1, t),
                          lambda t: half_block_out(2 * NBD - 1, t))
            boundary(U_X2, G_FFN2, S_FFN2, J_POSTM, EARLY_MIX)
            sum_up(J_IN2)
            ffn(S_FFN2, B_FFN2, U_H2, J_IN2, 1)
            down(S_DOWN2, B_FFN2 + 2 * FB, J_POST2, 1)
            rest(S_PROJ + 2, 2)
            update(J_POST2, 1, EARLY)
            rest(S_PROJ + 3, 3)
            for k in range(XU):
                if 0 < k < XU - 1:
                    update(J_POST2, k + 1, EARLY)
                if k < RING:
                    rest(S_GATE + k, k)
                x_rest_unit(U_PLE, k, G_PLE + CPS * k)
                if k >= RING:
                    rest(S_GATE + k, k % RING)
            sum_up(J_PLE)
            dve.wait_ge(ple_row_landed, 16)

            def gate_times_emb(nb, t):
                dve.wait_ge(sig_ready, T * nb + t + 1)
                if nb:
                    dve.wait_ge(squared, Q[J_POSTP] + T * (nb - 1) + t + 1)
                nc.vector.tensor_tensor(gated[:, t, :], sig[:, t, :], emb[:, t, blk(nb)], ALU.mult
                                        ).then_inc(gated_ready, 1)

            def times_gain_ple(nb, t):
                dve.wait_ge(gated_ready, T * nb + t + 1)
                return nc.vector.tensor_tensor(branch[:, t, blk(nb)], gated[:, t, :], ple_row[:, blk(nb)], ALU.mult)

            def final_update(t, nb):
                nc.vector.scalar_tensor_tensor(out=resid[:, t, blk(nb)], in0=branch[:, t, blk(nb)],
                                               scalar=rstd[:, J_POSTP, t:t + 1], in1=resid[:, t, blk(nb)],
                                               op0=ALU.mult, op1=ALU.add).then_inc(resid_ready, 1)

            for nb in range(NBD - 1):
                n = S_GATE + KS * nb
                ahead(n, 0 if nb else KS - RING, KS - 1 if nb else RING - 1)
                for t in range(T):
                    gate_times_emb(nb, t)
                for t in range(T):
                    ins = times_gain_ple(nb, t)
                ins.then_inc(branch_ready, 1)
                ahead(n, KS - 1, 1)
            ahead(S_GATE + KS * (NBD - 1), 0, KS - RING)
            gate_times_emb(NBD - 1, 0)
            step(times_gain_ple(NBD - 1, 0))
            sum_up(J_POSTP, 0, 1)
            dve.wait_ge(branch_ready, CREDIT + 4 * NBD - 1)
            dve.wait_ge(rstd_ready, factors_up_to(J_POSTP, 0))
            for nb in range(NBD):
                final_update(0, nb)
            gate_times_emb(NBD - 1, 1)
            times_gain_ple(NBD - 1, 1).then_inc(branch_ready, 1)
            sum_up(J_POSTP, 1, 2)
            dve.wait_ge(branch_ready, CREDIT + 4 * NBD)
            dve.wait_ge(rstd_ready, factors_up_to(J_POSTP))
            for nb in range(NBD):
                final_update(1, nb)


_OUT = (1, 256, 2048)


def kernel(**inputs):
    import numpy as _np
    import concourse.bacc as _bacc
    from concourse.bass_utils import run_bass_kernel_spmd as _run

    nc = _bacc.Bacc("TRN2", target_bir_lowering=False, num_devices=1)
    arrays, args = {}, {}
    for name, value in inputs.items():
        a = _np.ascontiguousarray(value)
        arrays[f"in_{name}"] = a
        args[name] = nc.dram_tensor(f"in_{name}", a.shape, mybir.dt.from_np(a.dtype), kind="ExternalInput").ap()
    out = nc.dram_tensor("out_h", _OUT, F32, kind="ExternalOutput").ap()
    layer_program(nc, out=out, **args)
    r = _run(nc, [arrays], core_ids=[0])
    return r.results[0]["out_h"]
```
